# Optimizing a Trainium2 kernel written in Bass

```python
import jax, jax.numpy as jnp
from jax import lax
import numpy as np

D_MODEL = 1024
BATCH = 1
SEQ = 1024
DEPTH = 1

CHUNK = 64
PLE_DIM = 256
NORM_EPS = 1e-6
NEG_INF = -1e30

GLA_HEADS = 4
GLA_DK = 128
GLA_DV = 256
GLA_GATE_RANK = 16
GLA_GATE_TEMP = 16.0

SWA_Q_HEADS = 16
SWA_KV_HEADS = 4
SWA_GROUP = SWA_Q_HEADS // SWA_KV_HEADS
SWA_HEAD_DIM = 64
SWA_WINDOW = 128
SWA_WINDOW_CHUNKS = SWA_WINDOW // CHUNK

PEER_HEADS = 8
PEER_NKEYS = 128
PEER_EXPERTS = PEER_NKEYS * PEER_NKEYS
PEER_QDIM = 256
PEER_HALF = PEER_QDIM // 2
PEER_TOPK = 16
PEER_TOKEN_BLOCK = 128

IN_SIZES = (GLA_HEADS * GLA_DK, GLA_HEADS * GLA_DK, GLA_HEADS * GLA_DV, GLA_HEADS * GLA_DV, GLA_GATE_RANK,
            SWA_Q_HEADS * SWA_HEAD_DIM, SWA_KV_HEADS * SWA_HEAD_DIM, SWA_KV_HEADS * SWA_HEAD_DIM)
IN_OFFSETS = tuple(sum(IN_SIZES[:i + 1]) for i in range(len(IN_SIZES) - 1))
IN_WIDTH = sum(IN_SIZES)

kernel_name = 'hybrid_gla_swa_peer_block'

def rmsnorm(x, g):
    xf = x.astype(jnp.float32)
    y = xf * lax.rsqrt(jnp.mean(xf * xf, axis=-1, keepdims=True) + NORM_EPS)
    return (y * g.astype(jnp.float32)).astype(x.dtype)

def alibi_slopes(n):
    return 2.0 ** (-8.0 * jnp.arange(1, n + 1, dtype=jnp.float32) / n)

def gla_branch(q, k, v, r, a_low, w_a2, b_a, g_onorm):
    f32 = jnp.float32
    Bb, S = q.shape[0], q.shape[1]
    nC = S // CHUNK
    log_a = jax.nn.log_sigmoid((a_low @ w_a2 + b_a).astype(f32)) / GLA_GATE_TEMP

    def chunks(t, d):
        return t.reshape(Bb, nC, CHUNK, GLA_HEADS, d).astype(f32)

    qc = chunks(q, GLA_DK) * (GLA_DK ** -0.5)
    kc = chunks(k, GLA_DK)
    vc = chunks(v, GLA_DV)
    la = chunks(log_a, GLA_DK)
    b = jnp.cumsum(la, axis=2)
    b_end = b[:, :, -1]
    k_dec = kc * jnp.exp(b_end[:, :, None] - b)
    U = jnp.einsum('bnchk,bnchv->bnhkv', k_dec, vc)

    def step(state, inp):
        decay, u, qch = inp
        state = jnp.exp(decay)[..., None] * state + u
        o = jnp.einsum('bchk,bhkv->bchv', qch, state)
        return state, o

    init = jnp.zeros((Bb, GLA_HEADS, GLA_DK, GLA_DV), f32)
    _, o = lax.scan(step, init, (jnp.swapaxes(b_end, 0, 1), jnp.swapaxes(U, 0, 1), jnp.swapaxes(qc, 0, 1)))
    o = jnp.swapaxes(o, 0, 1).reshape(Bb, S, GLA_HEADS, GLA_DV)
    o = rmsnorm(o, g_onorm) * jax.nn.silu(r.reshape(Bb, S, GLA_HEADS, GLA_DV).astype(f32))
    return o.reshape(Bb, S, GLA_HEADS * GLA_DV).astype(q.dtype)

def swa_branch(q, k, v, sinks):
    f32 = jnp.float32
    Bb, S = q.shape[0], q.shape[1]
    nC = S // CHUNK
    W = SWA_WINDOW_CHUNKS
    qc = q.reshape(Bb, nC, CHUNK, SWA_KV_HEADS, SWA_GROUP, SWA_HEAD_DIM)

    def band(t):
        tc = t.reshape(Bb, nC, CHUNK, SWA_KV_HEADS, SWA_HEAD_DIM)
        tp = jnp.pad(tc, ((0, 0), (W - 1, 0), (0, 0), (0, 0), (0, 0)))
        return jnp.concatenate([tp[:, j:j + nC] for j in range(W)], axis=2)

    kb = band(k)
    vb = band(v)
    logits = jnp.einsum('bnqhgd,bnkhd->bnhgqk', qc, kb).astype(f32) * (SWA_HEAD_DIM ** -0.5)
    qi = jnp.arange(CHUNK)
    kj = jnp.arange(W * CHUNK)
    ci = jnp.arange(nC)
    dist = jnp.abs((W - 1) * CHUNK + qi[:, None] - kj[None, :]).astype(f32)
    slopes = alibi_slopes(SWA_Q_HEADS).reshape(SWA_KV_HEADS, SWA_GROUP)
    logits = logits - slopes[:, :, None, None] * dist
    valid = (ci[:, None] * CHUNK + kj[None, :] - (W - 1) * CHUNK) >= 0
    logits = jnp.where(valid[None, :, None, None, None, :], logits, NEG_INF)
    sink = jnp.broadcast_to(sinks.astype(f32).reshape(SWA_KV_HEADS, SWA_GROUP)[:, :, None, None],
                            logits.shape[:-1] + (1,))
    probs = jax.nn.softmax(jnp.concatenate([logits, sink], axis=-1), axis=-1)[..., :-1]
    out = jnp.einsum('bnhgqk,bnkhd->bnqhgd', probs.astype(v.dtype), vb)
    return out.reshape(Bb, S, SWA_Q_HEADS * SWA_HEAD_DIM)

def peer_ffn(h, w_q, sub_keys, u_tab, v_tab):
    f32 = jnp.float32
    Bb, S, D = h.shape
    q = (h @ w_q).reshape(Bb, S, PEER_HEADS, 2, PEER_HALF)
    scores = jnp.einsum('bshpd,pnd->bshpn', q, sub_keys).astype(f32)
    vals, idx = lax.top_k(scores, PEER_TOPK)
    cand = vals[..., 0, :, None] + vals[..., 1, None, :]
    cidx = idx[..., 0, :, None] * PEER_NKEYS + idx[..., 1, None, :]
    cand = cand.reshape(Bb, S, PEER_HEADS, PEER_TOPK * PEER_TOPK)
    cidx = cidx.reshape(Bb, S, PEER_HEADS, PEER_TOPK * PEER_TOPK)
    top_vals, pos = lax.top_k(cand, PEER_TOPK)
    eidx = jnp.take_along_axis(cidx, pos, axis=-1)
    gates = jax.nn.softmax(top_vals, axis=-1)
    T = Bb * S
    nblk = T // PEER_TOKEN_BLOCK
    hb = h.reshape(nblk, PEER_TOKEN_BLOCK, D)
    eb = eidx.reshape(nblk, PEER_TOKEN_BLOCK, PEER_HEADS, PEER_TOPK)
    gb = gates.reshape(nblk, PEER_TOKEN_BLOCK, PEER_HEADS, PEER_TOPK)

    def block(args):
        xt, e, g = args
        u = jnp.take(u_tab, e, axis=0)
        act = jax.nn.gelu(jnp.einsum('td,thkd->thk', xt, u).astype(f32))
        vv = jnp.take(v_tab, e, axis=0)
        return jnp.einsum('thk,thkd->td', (g * act).astype(xt.dtype), vv)

    y = lax.map(block, (hb, eb, gb))
    return y.reshape(Bb, S, D)

def setup_inputs(seed: int = 0) -> dict:
    key = jax.random.key(seed)
    ks = jax.random.split(key, 24)
    f32 = jnp.float32
    L = DEPTH
    D = D_MODEL

    def nrm(k, shape, scale):
        return jax.random.normal(k, shape, f32) * scale

    def gain(k, shape):
        return 1.0 + 0.02 * jax.random.normal(k, shape, f32)

    return {
        'x': nrm(ks[0], (BATCH, SEQ, D), 1.0),
        'p': nrm(ks[1], (DEPTH, BATCH, SEQ, PLE_DIM), 1.0),
        'norm_mix': gain(ks[2], (L, D)),
        'w_in': nrm(ks[3], (L, D, IN_WIDTH), D ** -0.5),
        'w_gla_a2': nrm(ks[4], (L, GLA_GATE_RANK, GLA_HEADS * GLA_DK), GLA_GATE_RANK ** -0.5),
        'b_gla_a': 1.0 + nrm(ks[5], (L, GLA_HEADS * GLA_DK), 0.1),
        'gla_onorm': gain(ks[6], (L, GLA_DV)),
        'swa_sinks': nrm(ks[7], (L, SWA_Q_HEADS), 0.5),
        'w_gla_out': nrm(ks[8], (L, GLA_HEADS * GLA_DV, D), (GLA_HEADS * GLA_DV) ** -0.5),
        'w_swa_out': nrm(ks[9], (L, SWA_Q_HEADS * SWA_HEAD_DIM, D), (SWA_Q_HEADS * SWA_HEAD_DIM) ** -0.5),
        'w_branch_gate': nrm(ks[10], (L, D, 2 * D), D ** -0.5),
        'b_branch_gate': nrm(ks[11], (L, 2 * D), 0.02),
        'w_out': nrm(ks[12], (L, D, D), D ** -0.5),
        'norm_ffn': gain(ks[13], (L, D)),
        'peer_wq': nrm(ks[14], (L, D, PEER_HEADS * PEER_QDIM), D ** -0.5),
        'peer_subkeys': nrm(ks[15], (L, 2, PEER_NKEYS, PEER_HALF), PEER_HALF ** -0.5),
        'peer_u': nrm(ks[16], (L, PEER_EXPERTS, D), D ** -0.5),
        'peer_v': nrm(ks[17], (L, PEER_EXPERTS, D), 0.2),
        'norm_ple': gain(ks[18], (L, D)),
        'w_ple_gate': nrm(ks[19], (L, D, D), D ** -0.5),
        'w_ple_proj': nrm(ks[20], (L, PLE_DIM, D), PLE_DIM ** -0.5),
        'norm_final': gain(ks[21], (D,)),
    }

def reference(x, p, norm_mix, w_in, w_gla_a2, b_gla_a, gla_onorm, swa_sinks, w_gla_out, w_swa_out,
              w_branch_gate, b_branch_gate, w_out, norm_ffn, peer_wq, peer_subkeys, peer_u, peer_v,
              norm_ple, w_ple_gate, w_ple_proj, norm_final):
    for i in range(DEPTH):
        h = rmsnorm(x, norm_mix[i])
        proj = h @ w_in[i]
        gq, gk, gv, gr, ga, sq, sk, sv = jnp.split(proj, IN_OFFSETS, axis=-1)
        y_gla = gla_branch(gq, gk, gv, gr, ga, w_gla_a2[i], b_gla_a[i], gla_onorm[i]) @ w_gla_out[i]
        y_swa = swa_branch(sq, sk, sv, swa_sinks[i]) @ w_swa_out[i]
        gates = jax.nn.sigmoid((h @ w_branch_gate[i] + b_branch_gate[i]).astype(jnp.float32)).astype(x.dtype)
        g_gla, g_swa = jnp.split(gates, 2, axis=-1)
        x = x + (g_gla * y_gla + g_swa * y_swa) @ w_out[i]
        x = x + peer_ffn(rmsnorm(x, norm_ffn[i]), peer_wq[i], peer_subkeys[i], peer_u[i], peer_v[i])
        ple_gate = jax.nn.sigmoid((rmsnorm(x, norm_ple[i]) @ w_ple_gate[i]).astype(jnp.float32)).astype(x.dtype)
        x = x + ple_gate * (p[i] @ w_ple_proj[i])
    return rmsnorm(x, norm_final)


_drawn_inputs = setup_inputs


def setup_inputs(seed=0):
    import zlib

    import numpy as np

    out = dict(_drawn_inputs(seed))
    spreads = {}
    factors = {'norm_mix': 3.431,
     'b_gla_a': 2.963,
     'gla_onorm': 16.121,
     'swa_sinks': 64.0,
     'b_branch_gate': 8.0,
     'norm_ffn': 34.016,
     'norm_ple': 64.0,
     'norm_final': 7.544}
    for name, (base, spread) in spreads.items():
        noise = np.random.default_rng([zlib.crc32(name.encode()), seed]).standard_normal(out[name].shape)
        drawn = base * np.exp(spread * noise) if base else spread * noise
        out[name] = __import__('jax').numpy.asarray(drawn.astype(out[name].dtype))
    for name, factor in factors.items():
        out[name] = (out[name] * factor).astype(out[name].dtype)
    return out
```

```python
from contextlib import ExitStack

import numpy as np

import concourse.bass as bass
from concourse import mybir

ALU = mybir.AluOpType
ACT = mybir.ActivationFunctionType
AX = mybir.AxisListType
F32 = mybir.dt.float32
U32 = mybir.dt.uint32

P = 128
D = 1024
KT = D // P
SEQ = 1024
SEG = 512
NSEG = SEQ // SEG
TT = SEG // P
NTILE = SEQ // P
CHUNK = 64
EPS = 1e-6
PLE = 256

GH, GDK, GDV, GRANK, GTEMP = 4, 128, 256, 16, 16.0
QH, KVH, HD = 16, 4, 64
GROUP = QH // KVH
BAND = 3 * CHUNK
FAR = 1e33

NH, NK, TOPK = 8, 128, 16
NLIST = 2 * NH
LOW = -3.0e38

SW = 512
FRONT_SLABS = ["gk", "gv0", "gv1", "gq", "gr0", "gr1", "kv", "sq0", "sq1",
               "bgg0", "glo0", "bgs0", "swo0", "bgg1", "glo1", "bgs1", "swo1",
               "wo0", "wo1", "wq0", "wq1", "wq2", "wq3"]
TAIL_SLABS = ["pg0", "pg1", "pp"]
RS = 2
US, VS = 4, 8

SEG_PLAN = (
    [("turn h", "act", 8), ("ga", "act", 1), ("gate logits", "dve", TT), ("chunk sums", "act", 1),
     ("suffix sums", "act", TT), ("gk", "dve", TT), ("gv0", "act", TT), ("gv1", "act", TT), ("gq", "act", GH),
     ("gr0", "act", TT), ("gr1", "act", TT), ("turn linear o", "act", 2 * TT), ("kv", "act", 2 + TT),
     ("sq0", "act", 4), ("sq1", "act", 4), ("window", "act", 3 * TT * KVH)]
    + [(f"{w}{q}", e, 4) for q in range(2) for w, e in (("bgg", "act"), ("glo", "dve"), ("bgs", "act"), ("swo", "dve"))]
    + [("wo0", "dve", TT), ("wo1", "dve", TT), ("turn h2", "act", 8)]
    + [(w, "act", n) for q in range(4) for w, n in ((f"wq{q}", 4), ("scores", TT))])
TAIL_PLAN = [("turn h3", "act", 8), ("pg0", "act", TT), ("pg1", "act", TT), ("pp", "dve", 2 * TT)]
PLAN = SEG_PLAN * NSEG + TAIL_PLAN * NSEG
SEG_USES = [e for _, e, n in SEG_PLAN for _ in range(n)]
TAIL_USES = [e for _, e, n in TAIL_PLAN for _ in range(n)]
USES = SEG_USES * NSEG + TAIL_USES * NSEG
SLAB_READ = [sum(n for _, _, n in PLAN[:i + 1]) for i, (w, _, _) in enumerate(PLAN) if w in FRONT_SLABS + TAIL_SLABS]


def freed(n):
    return USES[n], USES[:n + 1].count(USES[n])


class Turn:

    def __init__(self, n=0):
        self.n = n

    def take(self):
        self.n += 1
        return self.n - 1


def build(nc, a, out):
    with ExitStack() as ctx:
        def sb(name, shape, dt=F32):
            return ctx.enter_context(nc.sbuf_tensor(name, shape, dt))

        def ps(name, shape):
            return ctx.enter_context(nc.psum_tensor(name, shape, F32))

        def sem(name):
            return ctx.enter_context(nc.semaphore(name))

        def dram(name, shape):
            return nc.dram_tensor(name, shape, F32, kind="Internal").ap()

        x1_d = dram("x1_d", (NTILE, P, D))
        h2_d = dram("h2_d", (NTILE, P, D))
        sc_d = dram("sc_d", (NTILE, P, NLIST * NK))
        x2_d = dram("x2_d", (NTILE, P, D))

        ident = sb("ident", [P, P])
        tri = sb("tri", [P, P])
        chunk_of = sb("chunk_of", [P, 2])
        dist = sb("dist", [P, 2, BAND])
        iota16 = sb("iota16", [P, TOPK])
        g_mix = sb("g_mix", [P, KT])
        g_ple = sb("g_ple", [P, KT])
        g_on = sb("g_on", [P, 2])
        b_bg = sb("b_bg", [P, 2 * KT])
        sinks = sb("sinks", [P, QH])
        g_ffn = sb("g_ffn", [P, D])
        wga = sb("wga", [P, KT, GRANK])
        wa2 = sb("wa2", [GRANK + 1, GH * GDK])
        subk = sb("subk", [P, 2, NK])
        eps = sb("eps", [P, 1])

        slab = sb("slab", [P, RS, KT * SW])
        hT = sb("hT", [P, KT, SEG])
        rX = sb("rX", [P, TT, D])
        rA = sb("rA", [P, 4096])
        rB = sb("rB", [P, 4096])
        rC = sb("rC", [P, 4096])
        rD = sb("rD", [P, 4096])
        rE = sb("rE", [P, TT, 512])
        gv = rA[:].rearrange("p (t n) -> p t n", t=TT)
        sqT = rA[:].rearrange("p (f n) -> p f n", f=8)
        gr = rB[:].rearrange("p (t n) -> p t n", t=TT)
        yswT = rB[:].rearrange("p (f n) -> p f n", f=8)
        ysc = rB[:].rearrange("p (b t n) -> p b t n", b=2, t=TT)
        yglT = rC[:].rearrange("p (f n) -> p f n", f=8)
        h2 = rC[:].rearrange("p (t n) -> p t n", t=TT)
        gqT = rD[:, 0:2048].rearrange("p (h n) -> p h n", h=GH)
        kdec = rD[:, 2048:4096].rearrange("p (t n) -> p t n", t=TT)
        mT = rD[:].rearrange("p (f n) -> p f n", f=8)
        skT = sb("skT", [P, 2, CHUNK + SEG])
        sv = sb("sv", [P, TT + 1, KVH * HD])
        aT = sb("aT", [GRANK + 1, SEG])
        dec = sb("dec", [P, GH, 2 * TT])
        state = sb("state", [P, 2, GH, GDV])
        stat = sb("stat", [P, 8, TT])
        gstat = sb("gstat", [P, 3, GH])
        otok = sb("otok", [P, GH * GDV])
        junk = sb("junk", [P, D])
        sl = sb("sl", [P, GROUP, BAND])
        sp_ = sb("sp_", [P, GROUP, 256])
        pT = sb("pT", [P, GROUP, 2, P])
        sm = sb("sm", [P, 6, GROUP])
        ubuf = hT[:].rearrange("p k n -> p (k n)").rearrange("p (s n) -> p s n", s=US)
        vbuf = rA[:].rearrange("p (s n) -> p s n", s=4)
        vbuf2 = rB[:].rearrange("p (s n) -> p s n", s=4)
        hn = rC[:, 0:1024]
        hc = rC[:, 1024:2048]
        acc = rC[:, 2048:3072]
        diag = rC[:, 3072:4096].rearrange("p (k n) -> p k n", k=8)
        sct = rD[:, 0:2048].rearrange("p (l n) -> p l n", l=NLIST)
        cand = rD[:, 2048:4096].rearrange("p (h n) -> p h n", h=NH)
        hot = rE[:].rearrange("p t n -> p (t n)").rearrange("p (h k i) -> p h k i", h=NH, k=TOPK)
        vals = sb("vals", [P, NLIST, TOPK])
        lidx = sb("lidx", [P, NLIST, TOPK], U32)
        lidf = sb("lidf", [P, NLIST, TOPK])
        tvals = sb("tvals", [P, NH, TOPK])
        pos = sb("pos", [P, NH, TOPK], U32)
        posi = sb("posi", [P, 2, NH, TOPK], U32)
        posf = sb("posf", [P, 2, NH, TOPK])
        picked = sb("picked", [P, 2, NH, TOPK])
        idx_next = sb("idx_next", [P, NH * TOPK], U32)
        idx_cur = sb("idx_cur", [P, NH * TOPK], U32)
        gate_next = sb("gate_next", [P, NH, TOPK])
        gate_cur = sb("gate_cur", [P, NH, TOPK])
        gsum = sb("gsum", [P, 2, NH])
        dots = sb("dots", [P, NH, TOPK])
        gel = sb("gel", [P, NH, TOPK])
        wts = sb("wts", [P, NH, TOPK])

        bank = ps("bank", [P, 4, 512])
        wide = ps("wide", [P, 4, 512])

        const_in = sem("const_in")
        x_in = sem("x_in")
        xres_in = sem("xres_in")
        slab_in = [sem(f"slab_in{i}") for i in range(RS)]
        bank_full = sem("bank_full")
        emptied = {"act": sem("emptied_act"), "dve": sem("emptied_dve")}
        squares_done = sem("squares_done")
        rstd_done = sem("rstd_done")
        root_done = sem("root_done")
        scaled = sem("scaled")
        gate_abs = sem("gate_abs")
        gate_ln = sem("gate_ln")
        log_a = sem("log_a")
        decay_exp = sem("decay_exp")
        u_full = sem("u_full")
        state_done = sem("state_done")
        o_full = sem("o_full")
        o_sq = sem("o_sq")
        o_root = sem("o_root")
        o_rstd = sem("o_rstd")
        o_gated = sem("o_gated")
        setup = sem("setup")
        carried = sem("carried")
        logit_full = sem("logit_full")
        logit_sb = sem("logit_sb")
        swa_step = sem("swa_step")
        swa_exp = sem("swa_exp")
        prob_ready = sem("prob_ready")
        prob_turned = sem("prob_turned")
        merge_step = sem("merge_step")
        x1_ready = sem("x1_ready")
        h2_gained = sem("h2_gained")
        act_step = sem("act_step")
        x1_out = sem("x1_out")
        h2_out = sem("h2_out")
        sc_out = [sem("sc_out0"), sem("sc_out1")]
        score_in = sem("score_in")
        h_in = sem("h_in")
        acc_in = sem("acc_in")
        topk_step = sem("topk_step")
        topk_exp = sem("topk_exp")
        h_copied = sem("h_copied")
        idx_ready = sem("idx_ready")
        held = sem("held")
        u_in = [sem(f"u_in{i}") for i in range(US)]
        v_in = [sem(f"v_in{i}") for i in range(VS)]
        u_used = sem("u_used")
        v_used_dve = sem("v_used_dve")
        v_used_pe = sem("v_used_pe")
        dots_done = sem("dots_done")
        gelu_done = sem("gelu_done")
        wts_done = sem("wts_done")
        diag_done = sem("diag_done")
        y_full = sem("y_full")
        x2_done = sem("x2_done")
        x2_out = sem("x2_out")
        tx_in = sem("tx_in")
        tp_in = sem("tp_in")
        tail_step = sem("tail_step")
        tail_out = sem("tail_out")

        NCONST = 14
        consts = [(ident[:], a["ident"]), (tri[:], a["tri"]), (chunk_of[:], a["chunk_of"]),
                  (dist[:], a["dist"]), (iota16[:], a["iota16"].partition_broadcast(P)),
                  (g_mix[:], a["g_mix"]), (g_ple[:], a["g_ple"]), (g_on[:], a["g_on"]),
                  (b_bg[:], a["b_bg"]), (sinks[:], a["sinks"].partition_broadcast(P)),
                  (g_ffn[:], a["g_ffn"].partition_broadcast(P)), (wga[:], a["wga"]),
                  (wa2[:], a["wa2"]), (subk[:], a["subk"])]
        assert len(consts) == NCONST
        CONST_READY = 16 * NCONST

        x_t = a["x"].rearrange("(t p) d -> p t d", p=P)
        out_t = out.rearrange("(t p) d -> p t d", p=P)
        n_front = len(FRONT_SLABS)
        n_tail = len(TAIL_SLABS)

        def slab_source(n):
            if n < NSEG * n_front:
                return a["slabs"][n % n_front]
            return a["slabs"][n_front + (n - NSEG * n_front) % n_tail]

        def slab_view(n):
            return slab[:, n % RS, :].rearrange("p (k n) -> p k n", k=KT)

        def vslot(s):
            return vbuf[:, s, :] if s < 4 else vbuf2[:, s - 4, :]

        block = ctx.enter_context(nc.Block())

        @block.sync
        def _(sp):
            for dst, src in consts:
                sp.dma_start(dst, src).then_inc(const_in, 16)

            def load_slab(n):
                if n >= RS:
                    sp.wait_ge(bank_full, SLAB_READ[n - RS])
                sp.dma_start(slab[:, n % RS, :], slab_source(n)).then_inc(slab_in[n % RS], 16)

            for s in range(NSEG):
                if s:
                    sp.wait_ge(h2_gained, TT * s)
                    sp.wait_ge(x1_out, 16 * s)
                sp.dma_start(rX[:], x_t[:, TT * s:TT * s + TT, :]).then_inc(x_in, 16)
                for j in range(n_front):
                    load_slab(s * n_front + j)
                    if j == 5:
                        sp.wait_ge(bank_full, s * len(SEG_USES) + 8)
                        sp.dma_start(rX[:], x_t[:, TT * s:TT * s + TT, :]).then_inc(xres_in, 16)
                    if j == 19:
                        sp.wait_ge(x1_ready, 2 * TT * (s + 1))
                        sp.dma_start(x1_d[TT * s:TT * s + TT].rearrange("t p d -> p t d"), rX[:]).then_inc(x1_out, 16)
                        sp.wait_ge(h2_gained, TT * (s + 1))
                        sp.dma_start(h2_d[TT * s:TT * s + TT].rearrange("t p d -> p t d"), h2).then_inc(h2_out, 16)
                for q in range(4):
                    first = s * len(SEG_USES) + len(SEG_USES) - (4 - q) * 8 + 7
                    sp.wait_ge(emptied["act"], freed(first)[1])
                    sp.dma_start(sc_d[TT * s:TT * s + TT, :, q * 512:q * 512 + 512].rearrange("t p n -> p t n"),
                                 ysc[:, q % 2]).then_inc(sc_out[q % 2], 16)

            sp.wait_ge(x1_out, 16 * NSEG)
            sp.wait_ge(h2_out, 16 * NSEG)
            for b in range(2):
                sp.wait_ge(sc_out[b], 32 * NSEG)
            sp.wait_ge(bank_full, NSEG * len(SEG_USES))
            sp.dma_start(sct, sc_d[0].rearrange("p (l n) -> p l n", l=NLIST)).then_inc(score_in, 16)
            sp.dma_start(hn, h2_d[0]).then_inc(h_in, 16)
            sp.dma_start(acc, x1_d[0]).then_inc(acc_in, 16)
            with sp.Fori(0, NTILE - 1) as i:
                sp.wait_ge(topk_step, i * TOPK_STEPS + TOPK_STEPS)
                sp.dma_start(sct, sc_d[bass.ds(i + 1, 1)].rearrange("o p (l n) -> p (o l) n", l=NLIST)).then_inc(score_in, 16)
                sp.wait_ge(h_copied, i + 1)
                sp.dma_start(hn, h2_d[bass.ds(i + 1, 1)].rearrange("o p n -> p (o n)")).then_inc(h_in, 16)
                sp.wait_ge(x2_done, i + 2)
                sp.dma_start(x2_d[bass.ds(i, 1)].rearrange("o p n -> p (o n)"), acc).then_inc(x2_out, 16)
                sp.wait_ge(x2_out, i * 16 + 16)
                sp.dma_start(acc, x1_d[bass.ds(i + 1, 1)].rearrange("o p n -> p (o n)")).then_inc(acc_in, 16)
            sp.wait_ge(x2_done, NTILE + 1)
            sp.dma_start(x2_d[NTILE - 1], acc).then_inc(x2_out, 16)
            sp.wait_ge(x2_out, 16 * NTILE)

            for s in range(NSEG):
                if s:
                    sp.wait_ge(tail_out, 16 * s)
                sp.dma_start(rX[:], x2_d[TT * s:TT * s + TT].rearrange("t p d -> p t d")).then_inc(tx_in, 16)
                if s:
                    sp.wait_ge(bank_full, NSEG * len(SEG_USES) + s * len(TAIL_USES))
                sp.dma_start(rE[:, 0:2, :], a["pT"][:, :, s * SEG:s * SEG + SEG]).then_inc(tp_in, 16)
                if s == 0:
                    sp.dma_start(g_ffn[:], a["g_fin"].partition_broadcast(P)).then_inc(tp_in, 16)
                for j in range(n_tail):
                    load_slab(NSEG * n_front + s * n_tail + j)
                sp.wait_ge(tail_step, TAIL_STEPS * (s + 1))
                sp.dma_start(out_t[:, TT * s:TT * s + TT, :], rX[:]).then_inc(tail_out, 16)
            sp.wait_ge(tail_out, 16 * NSEG)

        @block.gpsimd
        def _(pool):
            def hold(s, value):
                pool.wait_ge(s, value)
                pool.sem_inc(held, 1)

            def gather(table, row_slot, col, done):
                nc.gpsimd.indirect_dma_start(
                    out=row_slot, out_offset=None, in_=table,
                    in_offset=bass.IndirectOffsetOnAxis(ap=idx_cur[:, col:col + 1], axis=0)).then_inc(done, 16)

            with nc.gpsimd.Fori(0, NTILE) as i:
                hold(idx_ready, i + 1)
                for h in range(NH):
                    for k in range(TOPK):
                        n = h * TOPK + k
                        hold(u_used, i * (NH * TOPK) + n + 1)
                        gather(a["u"], ubuf[:, n % US, :], n, u_in[n % US])
                    for k in range(TOPK):
                        n = h * TOPK + k
                        if k % 2 == 0:
                            hold(v_used_dve, i * (NH * TOPK // 2) + n // 2 + 1)
                        else:
                            hold(v_used_pe, i * (NH * TOPK // 2) + n // 2 + 1)
                        gather(a["v"], vslot(n % VS), n, v_in[n % VS])

        @block.tensor
        def _(pe):
            turn = Turn()
            mm = nc.tensor.matmul

            def bank_for():
                n = turn.take()
                if n >= 4:
                    who, count = freed(n - 4)
                    pe.wait_ge(emptied[who], count)
                return bank[:, n % 4, :]

            def slab_for(n):
                pe.wait_ge(slab_in[n % RS], 16 * (n // RS + 1))
                return slab_view(n)

            def turned(src, tiles_ready, ready, base):
                for f in range(KT):
                    b = bank_for()
                    for t in range(TT):
                        if f == 0:
                            pe.wait_ge(ready, base + t + 1)
                        m = nc.tensor.transpose(b[:, t * P:t * P + P], src[:, t, f * P:f * P + P], ident[:])
                    m.then_inc(bank_full, 1)

            def by_feature(w, tiles, src, kt=KT, off=0):
                for f in tiles:
                    b = bank_for()
                    for k in range(kt):
                        m = mm(b, w[:, k, off + f * P:off + f * P + P], src[:, k, :], start=(k == 0), stop=(k == kt - 1))
                    m.then_inc(bank_full, 1)

            def by_token(w, cols, src, kt=KT, off=0):
                for t in range(TT):
                    b = bank_for()
                    for k in range(kt):
                        m = mm(b[:, 0:cols], src[:, k, t * P:t * P + P], w[:, k, off:off + cols],
                               start=(k == 0), stop=(k == kt - 1))
                    m.then_inc(bank_full, 1)

            pe.wait_ge(const_in, CONST_READY)
            pe.wait_ge(setup, SETUP)
            for s in range(NSEG):
                base = s * n_front
                u0 = s * len(SEG_USES)
                turned(rX, TT, scaled, s * 2 * TT)
                who, count = freed(u0 + 7)
                pe.wait_ge(emptied[who], count)
                b = bank_for()
                for k in range(KT):
                    m = mm(b[0:GRANK, :], wga[:, k, :], hT[:, k, :], start=(k == 0), stop=(k == KT - 1))
                m.then_inc(bank_full, 1)
                who, count = freed(u0 + 8)
                pe.wait_ge(emptied[who], count)
                for t in range(TT):
                    b = bank_for()
                    mm(b, aT[:, t * P:t * P + P], wa2[:], start=True, stop=True).then_inc(bank_full, 1)
                b = bank_for()
                for t in range(TT):
                    pe.wait_ge(log_a, s * TT + t + 1)
                    for h in range(GH):
                        c0 = h * 2 * TT + 2 * t
                        m = mm(b[:, c0:c0 + 2], rE[:, t, h * GDK:h * GDK + GDK], chunk_of[:], start=True, stop=True)
                m.then_inc(bank_full, 1)
                for t in range(TT):
                    b = bank_for()
                    mm(b, tri[:], rE[:, t, :], start=True, stop=True).then_inc(bank_full, 1)
                by_token(slab_for(base + 0), 512, hT)
                by_token(slab_for(base + 1), 512, hT)
                by_token(slab_for(base + 2), 512, hT)
                by_feature(slab_for(base + 3), range(4), hT)
                by_token(slab_for(base + 4), 512, hT)
                by_token(slab_for(base + 5), 512, hT)

                uw = wide[:, 0:2, :].rearrange("p b (h n) -> p (b h) n", h=2)
                ow = wide[:, 2:4, :].rearrange("p b (h n) -> p (b h) n", h=2)
                for t in range(TT):
                    for half in range(2):
                        c = 2 * t + half
                        r0 = half * CHUNK
                        if c == 0:
                            who, count = freed(turn.n - 1)
                            pe.wait_ge(emptied[who], count)
                            pe.wait_ge(emptied["dve"], USES[:turn.n].count("dve"))
                        for h in range(GH):
                            if c + s and h % 2 == 0:
                                pe.wait_ge(state_done, (s * 2 * TT + c - 1) * GH + h + 2)
                            m = mm(uw[:, h, :], kdec[r0:r0 + CHUNK, t, h * GDK:h * GDK + GDK],
                                   gv[r0:r0 + CHUNK, t, h * GDV:h * GDV + GDV], start=True, stop=True)
                            m.then_inc(u_full, 1)
                        if half == 0 and t + s:
                            pe.wait_ge(o_gated, (s * TT + t) * GH)
                        for h in range(GH):
                            pe.wait_ge(state_done, (s * 2 * TT + c) * GH + h + 1)
                            m = mm(ow[r0:r0 + CHUNK, h, :], gqT[:, h, c * CHUNK:c * CHUNK + CHUNK],
                                   state[:, c % 2, h, :], start=True, stop=True)
                            m.then_inc(o_full, 1)
                    pe.wait_ge(o_gated, (s * TT + t + 1) * GH)
                    for odd in range(2):
                        b = bank_for()
                        for j in range(4):
                            f = 2 * j + odd
                            m = nc.tensor.transpose(b[:, j * P:j * P + P], otok[:, f * P:f * P + P], ident[:])
                        m.then_inc(bank_full, 1)

                if s:
                    pe.wait_ge(carried, 2 * s)
                w = slab_for(base + 6)
                by_feature(w, range(2), hT)
                by_token(w, 256, hT, off=256)
                by_feature(slab_for(base + 7), range(4), hT)
                by_feature(slab_for(base + 8), range(4), hT)

                def logits(n):
                    t, g = divmod(n, KVH)
                    r0 = (g % 2) * HD
                    m0 = s * TT * KVH + n
                    if m0 >= 2:
                        pe.wait_ge(logit_sb, GROUP * (m0 - 1))
                    for j in range(GROUP):
                        f = (g // 2) * GROUP + j
                        o = wide[:, 2 * (n % 2) + j // 2, (j % 2) * BAND:(j % 2) * BAND + BAND]
                        m = mm(o, sqT[r0:r0 + HD, f, t * P:t * P + P],
                               skT[r0:r0 + HD, g // 2, t * P:t * P + BAND], start=True, stop=True)
                    m.then_inc(logit_full, 1)

                def values(n):
                    t, g = divmod(n, KVH)
                    r0 = (g % 2) * HD
                    m0 = s * TT * KVH + n
                    pe.wait_ge(prob_ready, m0 + 1)
                    for half in range(2):
                        b = bank_for()
                        for j in range(2):
                            for blk in range(2):
                                c0 = (2 * j + blk) * P
                                m = nc.tensor.transpose(b[:, c0:c0 + P],
                                                        sp_[:, 2 * half + j, blk * P:blk * P + P], ident[:])
                        m.then_inc(bank_full, 1)
                    pe.wait_ge(prob_turned, 2 * (m0 + 1))
                    b = bank_for()
                    for blk in range(2):
                        m = mm(b[r0:r0 + HD, :], sv[:, t + blk, g * HD:g * HD + HD], pT[:, :, blk, :],
                               start=(blk == 0), stop=(blk == 1))
                    m.then_inc(bank_full, 1)

                who, count = freed(turn.n - 1)
                pe.wait_ge(emptied[who], count)
                pe.wait_ge(state_done, (s + 1) * 2 * TT * GH)
                pe.wait_ge(o_gated, (s + 1) * TT * GH)
                logits(0)
                for n in range(TT * KVH):
                    if n + 1 < TT * KVH:
                        logits(n + 1)
                    values(n)

                who, count = freed(turn.n - 1)
                pe.wait_ge(emptied[who], count)
                for q in range(2):
                    for j, src in enumerate((hT, yglT, hT, yswT)):
                        by_feature(slab_for(base + 9 + 4 * q + j), range(4), src)
                pe.wait_ge(merge_step, MERGE_STEPS * (s + 1))
                for q in range(2):
                    by_token(slab_for(base + 17 + q), 512, mT)
                turned(h2, TT, h2_gained, s * TT)
                who, count = freed(turn.n - 1)
                pe.wait_ge(emptied[who], count)
                for q in range(4):
                    by_feature(slab_for(base + 19 + q), range(4), hT)
                    who, count = freed(turn.n - 1)
                    pe.wait_ge(emptied[who], count)
                    for t in range(TT):
                        b = bank_for()
                        for f in range(4):
                            m = mm(b[:, f * P:f * P + P], rE[:, f, t * P:t * P + P], subk[:, f % 2, :],
                                   start=True, stop=True)
                        m.then_inc(bank_full, 1)

            pe.wait_ge(logit_sb, NSEG * TT * KVH * GROUP)
            with pe.Fori(0, NTILE) as i:
                for h in range(NH):
                    for kk in range(TOPK // 2):
                        n = h * (TOPK // 2) + kk
                        k = 2 * kk + 1
                        if n == 0:
                            pe.wait_ge(x2_done, i + 1)
                        pe.wait_ge(diag_done, i * (NH * TOPK // 2) + n + 1)
                        pe.wait_ge(v_in[k % VS], (i * (NH * TOPK // VS) + (h * TOPK + k) // VS + 1) * 16)
                        for c in range(2):
                            m = mm(wide[:, c, :], diag[:, kk, :], vslot(k % VS)[:, c * 512:c * 512 + 512],
                                   start=(n == 0), stop=(n == NH * TOPK // 2 - 1))
                        m.then_inc(v_used_pe, 1)

            for s in range(NSEG):
                base = NSEG * n_front + s * n_tail
                turned(rA[:].rearrange("p (t n) -> p t n", t=TT), TT, scaled, NSEG * 2 * TT + s * 2 * TT)
                who, count = freed(turn.n - 1)
                pe.wait_ge(emptied[who], count)
                for q in range(2):
                    by_token(slab_for(base + q), 512, hT)
                pe.wait_ge(tp_in, 32 + 16 * s)
                w = slab[:, (base + 2) % RS, 0:2048].rearrange("p (k n) -> p k n", k=2)
                slab_for(base + 2)
                by_token(w, 512, rE, kt=2, off=0)
                by_token(w, 512, rE, kt=2, off=512)

        @block.scalar
        def _(act):
            turn = Turn()
            fn = nc.scalar.activation

            def full():
                n = turn.take()
                act.wait_ge(bank_full, n + 1)
                return bank[:, n % 4, :]

            def skip(k):
                for _ in range(k):
                    turn.take()

            def norm_rows(src, dst, count):
                for t in range(TT):
                    if t or count:
                        act.wait_ge(squares_done, count * TT + t)
                    fn(junk[:], src[:, t, :], ACT.Square, accum_out=stat[:, 0, t:t + 1]).then_inc(squares_done, 1)
                act.wait_ge(squares_done, count * TT + TT)
                fn(stat[:, 1, :], stat[:, 0, :], ACT.Sqrt, bias=eps[:], scale=1.0 / D).then_inc(root_done, 1)
                act.wait_ge(rstd_done, count + 1)
                for t in range(TT):
                    fn(dst[:, t, :], src[:, t, :], ACT.Copy, scale=stat[:, 2, t:t + 1]).then_inc(scaled, 1)

            act.wait_ge(const_in, CONST_READY)
            act.wait_ge(setup, SETUP)
            for s in range(NSEG):
                u0 = s * len(SEG_USES)
                act.wait_ge(x_in, 16 * (s + 1))
                norm_rows(rX, rX, 2 * s)
                if s:
                    act.wait_ge(bank_full, u0)
                for f in range(KT):
                    fn(hT[:, f, :], full(), ACT.Copy, scale=g_mix[:, f:f + 1]).then_inc(emptied["act"], 1)
                fn(aT[0:GRANK, :], full()[0:GRANK, :], ACT.Copy).then_inc(emptied["act"], 1)
                for t in range(TT):
                    b = full()
                    fn(rE[:, t, :], b, ACT.Abs).then_inc(gate_abs, 1)
                for t in range(TT):
                    act.wait_ge(gate_abs, 3 * TT * s + t + 1)
                    fn(rE[:, t, :], rE[:, t, :], ACT.Exp, scale=-1.0).then_inc(gate_abs, 1)
                for t in range(TT):
                    act.wait_ge(gate_abs, 3 * TT * s + TT + t + 1)
                    fn(rE[:, t, :], rE[:, t, :], ACT.Ln, bias=1.0).then_inc(gate_abs, 1)
                b = full()
                if s:
                    act.wait_ge(state_done, s * 2 * TT * GH)
                fn(dec[:].rearrange("p h c -> p (h c)"), b[:, 0:GH * 2 * TT], ACT.Exp,
                   scale=1.0 / GTEMP).then_inc(emptied["act"], 1)
                for t in range(TT):
                    fn(rE[:, t, :], full(), ACT.Exp, scale=1.0 / GTEMP).then_inc(emptied["act"], 1)
                skip(TT)
                for half in range(2):
                    for t in range(TT):
                        fn(gv[:, t, half * 512:half * 512 + 512], full(), ACT.Copy).then_inc(emptied["act"], 1)
                for h in range(GH):
                    fn(gqT[:, h, :], full(), ACT.Copy, scale=GDK ** -0.5).then_inc(emptied["act"], 1)
                if s:
                    for b2 in range(2):
                        act.wait_ge(sc_out[b2], 32 * s)
                for half in range(2):
                    for t in range(TT):
                        fn(gr[:, t, half * 512:half * 512 + 512], full(), ACT.Silu).then_inc(emptied["act"], 1)

                ow = wide[:, 2:4, :].rearrange("p b (h n) -> p (b h) n", h=2)
                if s:
                    act.wait_ge(h2_out, 16 * s)
                for t in range(TT):
                    act.wait_ge(o_full, (s * TT + t + 1) * 2 * GH)
                    m0 = s * TT + t
                    for h in range(GH):
                        if h or m0:
                            act.wait_ge(o_sq, m0 * GH + h)
                        fn(junk[:, 0:GDV], ow[:, h, :], ACT.Square, accum_out=gstat[:, 0, h:h + 1]).then_inc(o_sq, 1)
                    act.wait_ge(o_sq, m0 * GH + GH)
                    fn(gstat[:, 1, :], gstat[:, 0, :], ACT.Sqrt, bias=eps[:], scale=1.0 / GDV).then_inc(o_root, 1)
                    for odd in range(2):
                        b = full()
                        fn(yglT[:, odd:8:2, t * P:t * P + P], b.rearrange("p (f n) -> p f n", f=4), ACT.Copy,
                           scale=g_on[:, odd:odd + 1]).then_inc(emptied["act"], 1)

                if s:
                    act.wait_ge(carried, 2 * s)
                for f in range(2):
                    fn(skT[:, f, CHUNK:], full(), ACT.Copy).then_inc(emptied["act"], 1)
                for t in range(TT):
                    fn(sv[:, t + 1, :], full()[:, 0:KVH * HD], ACT.Copy).then_inc(emptied["act"], 1)
                for f in range(8):
                    fn(sqT[:, f, :], full(), ACT.Copy, scale=HD ** -0.5).then_inc(emptied["act"], 1)
                for n in range(TT * KVH):
                    t, g = divmod(n, KVH)
                    m0 = s * TT * KVH + n
                    r0 = (g % 2) * HD
                    act.wait_ge(swa_step, SWA_STEPS * m0 + 3)
                    if m0:
                        act.wait_ge(bank_full, turn.n)
                    for j in range(GROUP):
                        fn(sp_[:, j, CHUNK:256], sl[:, j, :], ACT.Exp, bias=sm[:, 1, j:j + 1],
                           accum_out=sm[:, 3, j:j + 1]).then_inc(swa_exp, 1)
                    fn(sm[:, 4, :], sm[:, 2, :], ACT.Exp).then_inc(swa_exp, 1)
                    for half in range(2):
                        b = full()
                        if m0 and half == 0:
                            act.wait_ge(bank_full, turn.n - 1)
                        fn(pT[:, 2 * half:2 * half + 2, :, :].rearrange("p j b n -> p (j b n)"), b,
                           ACT.Copy).then_inc(prob_turned, 1)
                        act.wait_ge(prob_turned, 2 * m0 + half + 1)
                        act.sem_inc(emptied["act"], 1)
                    b = full()
                    fn(yswT[r0:r0 + HD, (g // 2) * GROUP:(g // 2) * GROUP + GROUP, t * P:t * P + P],
                       b[r0:r0 + HD, :].rearrange("p (j n) -> p j n", j=GROUP), ACT.Copy).then_inc(emptied["act"], 1)

                for q in range(2):
                    for br in range(2):
                        for f in range(4):
                            b = full()
                            if s or q or br:
                                act.wait_ge(merge_step, MERGE_STEPS * s + 12 * q + 4 * br)
                            fn(rE[:, f, :], b, ACT.Sigmoid, bias=b_bg[:, br * 8 + 4 * q + f:br * 8 + 4 * q + f + 1]
                               ).then_inc(emptied["act"], 1)
                        skip(4)
                skip(2 * TT)
                act.wait_ge(x1_ready, 2 * TT * (s + 1))
                norm_rows(rX, h2, 2 * s + 1)
                for f in range(KT):
                    fn(hT[:, f, :], full(), ACT.Copy).then_inc(emptied["act"], 1)
                for q in range(4):
                    if q:
                        act.wait_ge(bank_full, turn.n)
                    for f in range(4):
                        fn(rE[:, f, :], full(), ACT.Copy).then_inc(emptied["act"], 1)
                    if q >= 2:
                        act.wait_ge(sc_out[q % 2], 32 * s + 16)
                    for t in range(TT):
                        fn(ysc[:, q % 2, t, :], full(), ACT.Copy).then_inc(emptied["act"], 1)

            def softmax_exp(tile_steps, count):
                act.wait_ge(topk_step, tile_steps)
                fn(gate_next[:].rearrange("p h k -> p (h k)"), tvals[:].rearrange("p h k -> p (h k)"),
                   ACT.Exp).then_inc(topk_exp, 1)

            def peer_tile(i, last):
                act.wait_ge(h_in, i * 16 + 16)
                act.wait_ge(dots_done, i * NH + 1)
                fn(hc, hn, ACT.Copy).then_inc(h_copied, 1)
                for h in range(NH):
                    act.wait_ge(dots_done, i * NH + h + 2)
                    fn(gel[:, h, :], dots[:, h, :], ACT.Gelu_apprx_tanh).then_inc(gelu_done, 1)
                    act.wait_ge(wts_done, i * NH + h + 1)
                    for kk in range(TOPK // 2):
                        k = 2 * kk + 1
                        if h:
                            act.wait_ge(v_used_pe, i * (NH * TOPK // 2) + (h - 1) * (TOPK // 2) + kk + 1 + VS // 2)
                        elif kk == 0:
                            act.wait_ge(x2_done, i + 1)
                        fn(diag[:, kk, :], ident[:], ACT.Copy, scale=wts[:, h, k:k + 1]).then_inc(diag_done, 1)
                    if h == 6 and not last:
                        softmax_exp((i + 1) * TOPK_STEPS + EXP_AT, i)

            softmax_exp(EXP_AT, 0)
            with act.Fori(0, NTILE - 1) as i:
                peer_tile(i, False)
            peer_tile(NTILE - 1, True)

            hs = rA[:].rearrange("p (t n) -> p t n", t=TT)
            gates = rB[:].rearrange("p (q t n) -> p q t n", q=2, t=TT)
            for s in range(NSEG):
                act.wait_ge(tx_in, 16 * (s + 1))
                if s:
                    act.wait_ge(bank_full, turn.n)
                norm_rows(rX, hs, 2 * NSEG + 2 * s)
                for f in range(KT):
                    fn(hT[:, f, :], full(), ACT.Copy, scale=g_ple[:, f:f + 1]).then_inc(emptied["act"], 1)
                for q in range(2):
                    for t in range(TT):
                        b = full()
                        if s:
                            act.wait_ge(tail_step, TAIL_STEPS * s)
                        fn(gates[:, q, t, :], b, ACT.Sigmoid).then_inc(emptied["act"], 1)
                skip(2 * TT)
                act.wait_ge(tail_step, TAIL_STEPS * s + 2 * TT)
                norm_rows(rX, rX, 2 * NSEG + 2 * s + 1)

        @block.vector
        def _(dve):
            v = nc.vector
            turn = Turn()

            def full():
                n = turn.take()
                dve.wait_ge(bank_full, n + 1)
                return bank[:, n % 4, :]

            def skip(k):
                for _ in range(k):
                    turn.take()

            def rstd(count):
                dve.wait_ge(root_done, count + 1)
                v.reciprocal(stat[:, 2, :], stat[:, 1, :]).then_inc(rstd_done, 1)

            v.memset(eps[:], EPS).then_inc(setup, 1)
            v.memset(aT[:], 1.0).then_inc(setup, 1)
            v.memset(skT[:, :, 0:CHUNK], 0.0).then_inc(setup, 1)
            v.memset(sv[:, 0, :], 0.0).then_inc(setup, 1)
            v.memset(sp_[:], 0.0).then_inc(setup, 1)
            v.memset(state[:, 1], 0.0).then_inc(setup, 1)
            dve.sem_inc(u_used, US)
            dve.sem_inc(v_used_dve, VS // 2)
            dve.sem_inc(v_used_pe, VS // 2)
            dve.sem_inc(dots_done, 1)
            dve.sem_inc(x2_done, 1)
            dve.wait_ge(setup, SETUP)
            dve.wait_ge(const_in, CONST_READY)
            for s in range(NSEG):
                rstd(2 * s)
                skip(9)
                for t in range(TT):
                    b = full()
                    dve.wait_ge(gate_abs, 3 * TT * s + 2 * TT + t + 1)
                    v.scalar_tensor_tensor(out=rE[:, t, :], in0=b, scalar=0.0, in1=rE[:, t, :], op0=ALU.min,
                                           op1=ALU.subtract).then_inc(log_a, 1)
                    dve.wait_ge(log_a, s * TT + t + 1)
                    dve.sem_inc(emptied["dve"], 1)
                skip(TT + 1)
                for t in range(TT):
                    b = full()
                    who, count = freed(s * len(SEG_USES) + 14 + t)
                    dve.wait_ge(emptied[who], count)
                    v.tensor_tensor(kdec[:, t, :], b, rE[:, t, :], ALU.mult).then_inc(emptied["dve"], 1)
                skip(2 * TT + GH + 2 * TT)
                uw = wide[:, 0:2, :].rearrange("p b (h n) -> p (b h) n", h=2)
                ow = wide[:, 2:4, :].rearrange("p b (h n) -> p (b h) n", h=2)
                who, count = freed(s * len(SEG_USES) + 13)
                dve.wait_ge(emptied[who], count)
                for t in range(TT):
                    for half in range(2):
                        c = 2 * t + half
                        m0 = (s * 2 * TT + c) * GH
                        for h in range(GH):
                            dve.wait_ge(u_full, m0 + h // 2 * 2 + 2)
                            if m0:
                                dve.wait_ge(state_done, m0 - GH + h + 1)
                            if m0 >= 2 * GH:
                                dve.wait_ge(o_full, m0 - 2 * GH + h + 1)
                            v.scalar_tensor_tensor(out=state[:, c % 2, h, :], in0=state[:, 1 - c % 2, h, :],
                                                   scalar=dec[:, h, c:c + 1], in1=uw[:, h, :], op0=ALU.mult,
                                                   op1=ALU.add).then_inc(state_done, 1)
                    m1 = s * TT + t
                    dve.wait_ge(o_root, m1 + 1)
                    v.reciprocal(gstat[:, 2, :], gstat[:, 1, :]).then_inc(o_rstd, 1)
                    dve.wait_ge(o_rstd, m1 + 1)
                    dve.wait_ge(bank_full, turn.n + 2 * t)
                    who, count = freed(turn.n - 1)
                    dve.wait_ge(emptied[who], count)
                    for h in range(GH):
                        v.scalar_tensor_tensor(out=otok[:, h * GDV:h * GDV + GDV], in0=ow[:, h, :],
                                               scalar=gstat[:, 2, h:h + 1], in1=gr[:, t, h * GDV:h * GDV + GDV],
                                               op0=ALU.mult, op1=ALU.mult).then_inc(o_gated, 1)
                skip(2 * TT)
                skip(2 + TT + 8)
                for n in range(TT * KVH):
                    t, g = divmod(n, KVH)
                    m0 = s * TT * KVH + n
                    d0 = SWA_STEPS * m0
                    dve.wait_ge(logit_full, m0 + 1)
                    if m0:
                        dve.wait_ge(swa_exp, (GROUP + 1) * m0)
                    for j in range(GROUP):
                        slope = 2.0 ** (-8.0 * (g * GROUP + j + 1) / QH)
                        v.scalar_tensor_tensor(out=sl[:, j, :], in0=dist[:, 0 if m0 < KVH else 1, :], scalar=-slope,
                                               in1=wide[:, 2 * (n % 2) + j // 2, (j % 2) * BAND:(j % 2) * BAND + BAND],
                                               op0=ALU.mult, op1=ALU.add).then_inc(logit_sb, 1)
                    dve.wait_ge(logit_sb, GROUP * (m0 + 1))
                    v.tensor_reduce(sm[:, 0, :], sl[:], AX.X, ALU.max).then_inc(swa_step, 1)
                    dve.wait_ge(swa_step, d0 + 1)
                    v.tensor_tensor(sm[:, 5, :], sm[:, 0, :], sinks[:, g * GROUP:g * GROUP + GROUP],
                                    ALU.max).then_inc(swa_step, 1)
                    dve.wait_ge(swa_step, d0 + 2)
                    v.tensor_tensor(sm[:, 2, :], sinks[:, g * GROUP:g * GROUP + GROUP], sm[:, 5, :], ALU.subtract)
                    v.tensor_scalar(sm[:, 1, :], sm[:, 5, :], -1.0, None, ALU.mult).then_inc(swa_step, 1)
                    dve.wait_ge(swa_exp, (GROUP + 1) * (m0 + 1))
                    v.tensor_tensor(sm[:, 3, :], sm[:, 3, :], sm[:, 4, :], ALU.add).then_inc(swa_step, 1)
                    dve.wait_ge(swa_step, d0 + 4)
                    v.reciprocal(sm[:, 5, :], sm[:, 3, :]).then_inc(swa_step, 1)
                    dve.wait_ge(swa_step, d0 + 5)
                    v.tensor_tensor(sp_[:, :, CHUNK:256], sp_[:, :, CHUNK:256],
                                    sm[:, 5, :].unsqueeze(2).broadcast_to([P, GROUP, BAND]),
                                    ALU.mult).then_inc(prob_ready, 1)
                skip(3 * TT * KVH)
                if s + 1 < NSEG:
                    dve.wait_ge(bank_full, turn.n)
                    v.tensor_copy(skT[:, :, 0:CHUNK], skT[:, :, SEG:SEG + CHUNK]).then_inc(carried, 1)
                    v.tensor_copy(sv[:, 0, :], sv[:, TT, :]).then_inc(carried, 1)

                for q in range(2):
                    b0 = MERGE_STEPS * s + 12 * q
                    skip(4)
                    for f in range(4):
                        b = full()
                        who, count = freed(turn.n - 1 - f - 1)
                        dve.wait_ge(emptied[who], count)
                        v.tensor_tensor(mT[:, 4 * q + f, :], b, rE[:, f, :], ALU.mult).then_inc(merge_step, 1)
                        dve.wait_ge(merge_step, b0 + f + 1)
                        dve.sem_inc(emptied["dve"], 1)
                    skip(4)
                    for f in range(4):
                        b = full()
                        who, count = freed(turn.n - 1 - f - 1)
                        dve.wait_ge(emptied[who], count)
                        v.tensor_tensor(rE[:, f, :], b, rE[:, f, :], ALU.mult).then_inc(merge_step, 1)
                        dve.wait_ge(merge_step, b0 + 4 + 2 * f + 1)
                        dve.sem_inc(emptied["dve"], 1)
                        v.tensor_tensor(mT[:, 4 * q + f, :], mT[:, 4 * q + f, :], rE[:, f, :],
                                        ALU.add).then_inc(merge_step, 1)
                dve.wait_ge(xres_in, 16 * (s + 1))
                for q in range(2):
                    for t in range(TT):
                        b = full()
                        v.tensor_tensor(rX[:, t, q * 512:q * 512 + 512], rX[:, t, q * 512:q * 512 + 512], b,
                                        ALU.add).then_inc(x1_ready, 1)
                        dve.wait_ge(x1_ready, s * 2 * TT + q * TT + t + 1)
                        dve.sem_inc(emptied["dve"], 1)
                rstd(2 * s + 1)
                for t in range(TT):
                    dve.wait_ge(scaled, s * 2 * TT + TT + t + 1)
                    v.tensor_tensor(h2[:, t, :], h2[:, t, :], g_ffn[:], ALU.mult).then_inc(h2_gained, 1)
                skip(8 + 4 * (4 + TT))

            def step(base, n):
                dve.wait_ge(topk_step, base + n)
                dve.sem_inc(held, 1)

            def top16(lists, rows, out_vals, out_idx, base, n):
                for l in lists:
                    m = v.max(out_vals[:, l, 0:8], rows[:, l, :])
                m.then_inc(topk_step, 1)
                step(base, n + 1)
                for l in lists:
                    m = v.max_index(out_idx[:, l, 0:8], out_vals[:, l, 0:8], rows[:, l, :])
                m.then_inc(topk_step, 1)
                step(base, n + 2)
                for l in lists:
                    m = v.match_replace(rows[:, l, :], out_vals[:, l, 0:8], rows[:, l, :], LOW)
                m.then_inc(topk_step, 1)
                step(base, n + 3)
                for l in lists:
                    m = v.max(out_vals[:, l, 8:16], rows[:, l, :])
                m.then_inc(topk_step, 1)
                step(base, n + 4)
                for l in lists:
                    m = v.max_index(out_idx[:, l, 8:16], out_vals[:, l, 8:16], rows[:, l, :])
                m.then_inc(topk_step, 1)
                step(base, n + 5)

            def topk_part(part, i):
                base = i * TOPK_STEPS
                if part < 4:
                    if part == 0:
                        dve.wait_ge(score_in, i * 16 + 16)
                        dve.sem_inc(held, 1)
                    top16(range(4 * part, 4 * part + 4), sct, vals, lidx, base, 5 * part)
                elif part == 4:
                    lists = vals[:].rearrange("p (h q) k -> p h q k", q=2)
                    v.tensor_tensor(cand.rearrange("p h (i j) -> p h i j", i=TOPK),
                                    lists[:, :, 0, :].unsqueeze(3).broadcast_to([P, NH, TOPK, TOPK]),
                                    lists[:, :, 1, :].unsqueeze(2).broadcast_to([P, NH, TOPK, TOPK]),
                                    ALU.add).then_inc(topk_step, 1)
                    step(base, 21)
                    top16(range(0, 4), cand, tvals, pos, base, 21)
                elif part == 5:
                    top16(range(4, 8), cand, tvals, pos, base, 26)
                    v.tensor_copy(lidf[:], lidx[:])
                    v.tensor_scalar(posi[:, 0], pos[:], 4, None, ALU.logical_shift_right)
                    v.tensor_scalar(posi[:, 1], pos[:], 15, None, ALU.bitwise_and).then_inc(topk_step, 1)
                    step(base, 32)
                    v.tensor_copy(posf[:], posi[:])
                    v.tensor_copy(gsum[:, 0, :], tvals[:, :, 0]).then_inc(topk_step, 1)
                    step(base, 33)
                    v.tensor_tensor(tvals[:], tvals[:], gsum[:, 0, :].unsqueeze(2).broadcast_to([P, NH, TOPK]),
                                    ALU.subtract).then_inc(topk_step, 1)
                    step(base, 34)
                elif part == 6:
                    keys = lidf[:].rearrange("p (h q) k -> p h q k", q=2)
                    for q in range(2):
                        n = 34 + 3 * q
                        v.tensor_tensor(hot, iota16[:].unsqueeze(1).unsqueeze(1).broadcast_to([P, NH, TOPK, TOPK]),
                                        posf[:, q].unsqueeze(3).broadcast_to([P, NH, TOPK, TOPK]),
                                        ALU.is_equal).then_inc(topk_step, 1)
                        step(base, n + 1)
                        v.tensor_tensor(hot, hot, keys[:, :, q, :].unsqueeze(2).broadcast_to([P, NH, TOPK, TOPK]),
                                        ALU.mult).then_inc(topk_step, 1)
                        step(base, n + 2)
                        v.tensor_reduce(picked[:, q].rearrange("p h k -> p (h k)"),
                                        hot.rearrange("p h k i -> p (h k) i"), AX.X, ALU.add).then_inc(topk_step, 1)
                        step(base, n + 3)
                else:
                    v.scalar_tensor_tensor(out=idx_next[:], in0=picked[:, 0].rearrange("p h k -> p (h k)"),
                                           scalar=float(NK), in1=picked[:, 1].rearrange("p h k -> p (h k)"),
                                           op0=ALU.mult, op1=ALU.add)
                    dve.wait_ge(topk_exp, i + 1)
                    dve.sem_inc(held, 1)
                    v.tensor_reduce(gsum[:, 0, :], gate_next[:], AX.X, ALU.add).then_inc(topk_step, 1)
                    step(base, 41)
                    v.reciprocal(gsum[:, 1, :], gsum[:, 0, :]).then_inc(topk_step, 1)
                    step(base, 42)
                    v.tensor_tensor(gate_next[:], gate_next[:], gsum[:, 1, :].unsqueeze(2).broadcast_to([P, NH, TOPK]),
                                    ALU.mult).then_inc(topk_step, 1)
                    step(base, 43)

            def peer_tile(i, last):
                v.tensor_copy(gate_cur[:], gate_next[:])
                v.tensor_copy(idx_cur[:], idx_next[:]).then_inc(idx_ready, 1)
                dve.wait_ge(h_copied, i + 1)
                for h in range(NH):
                    for k in range(TOPK):
                        n = h * TOPK + k
                        row = ubuf[:, n % US, :]
                        dve.wait_ge(u_in[n % US], (i * (NH * TOPK // US) + n // US + 1) * 16)
                        v.scalar_tensor_tensor(out=row, in0=row, scalar=1.0, in1=hc, op0=ALU.mult, op1=ALU.mult,
                                               accum_out=dots[:, h, k:k + 1]).then_inc(u_used, 1)
                    dve.wait_ge(u_used, i * (NH * TOPK) + (h + 1) * TOPK + US)
                    dve.sem_inc(dots_done, 1)
                    if not last:
                        topk_part(h, i + 1)
                    dve.wait_ge(gelu_done, i * NH + h + 1)
                    dve.wait_ge(idx_ready, i + 1)
                    v.tensor_tensor(wts[:, h, :], gel[:, h, :], gate_cur[:, h, :], ALU.mult).then_inc(wts_done, 1)
                    dve.wait_ge(wts_done, i * NH + h + 1)
                    for kk in range(TOPK // 2):
                        k = 2 * kk
                        n = h * (TOPK // 2) + kk
                        if n == 0:
                            dve.wait_ge(acc_in, i * 16 + 16)
                        dve.wait_ge(v_used_dve, i * (NH * TOPK // 2) + n + VS // 2)
                        dve.wait_ge(v_in[k % VS], (i * (NH * TOPK // VS) + (h * TOPK + k) // VS + 1) * 16)
                        v.scalar_tensor_tensor(out=acc, in0=vslot(k % VS), scalar=wts[:, h, k:k + 1], in1=acc,
                                               op0=ALU.mult, op1=ALU.add).then_inc(v_used_dve, 1)
                dve.wait_ge(v_used_dve, (i + 1) * (NH * TOPK // 2) + VS // 2)
                dve.wait_ge(v_used_pe, (i + 1) * (NH * TOPK // 2) + VS // 2)
                v.tensor_tensor(acc.rearrange("p (c n) -> p c n", c=2), acc.rearrange("p (c n) -> p c n", c=2),
                                wide[:, 0:2, :], ALU.add).then_inc(x2_done, 1)

            dve.wait_ge(score_in, 16)
            for part in range(NH):
                topk_part(part, 0)
            with v.Fori(0, NTILE - 1) as i:
                peer_tile(i, False)
            peer_tile(NTILE - 1, True)

            gates = rB[:].rearrange("p (q t n) -> p q t n", q=2, t=TT)
            dve.wait_ge(tp_in, 32)
            for s in range(NSEG):
                rstd(2 * NSEG + 2 * s)
                skip(8 + 2 * TT)
                for q in range(2):
                    for t in range(TT):
                        b = full()
                        n = q * TT + t
                        who, count = freed(NSEG * len(SEG_USES) + s * len(TAIL_USES) + 8 + n)
                        dve.wait_ge(emptied[who], count)
                        v.tensor_tensor(gates[:, q, t, :], b, gates[:, q, t, :], ALU.mult).then_inc(emptied["dve"], 1)
                        who, count = freed(turn.n - 1)
                        dve.wait_ge(emptied["dve"], count)
                        v.tensor_tensor(rX[:, t, q * 512:q * 512 + 512], rX[:, t, q * 512:q * 512 + 512],
                                        gates[:, q, t, :], ALU.add).then_inc(tail_step, 1)
                rstd(2 * NSEG + 2 * s + 1)
                for t in range(TT):
                    dve.wait_ge(scaled, NSEG * 2 * TT + s * 2 * TT + TT + t + 1)
                    v.tensor_tensor(rX[:, t, :], rX[:, t, :], g_ffn[:], ALU.mult).then_inc(tail_step, 1)


SETUP = 6
SWA_STEPS = 5
MERGE_STEPS = 24
TOPK_STEPS = 43
EXP_AT = 34
TAIL_STEPS = 2 * TT + TT


def shape_tables():
    q = np.arange(P)[:, None]
    k = np.arange(P)[None, :]
    tri = ((q // CHUNK == k // CHUNK) & (q > k)).astype(np.float32)
    chunk_of = (q // CHUNK == np.arange(2)[None, :]).astype(np.float32)
    col = np.arange(BAND)[None, :]
    near = (col // CHUNK == q // CHUNK) | (col // CHUNK == q // CHUNK + 1)
    far = np.abs(q - (col - CHUNK)).astype(np.float32)
    later = np.where(near, far, FAR).astype(np.float32)
    first = np.where(near & (col >= CHUNK), far, FAR).astype(np.float32)
    return {"ident": np.eye(P, dtype=np.float32), "tri": tri, "chunk_of": chunk_of,
            "dist": np.stack([first, later], 1), "iota16": np.arange(TOPK, dtype=np.float32)}


def kernel(**inputs):
    import concourse.bacc as bacc
    from concourse.bass_utils import run_bass_kernel_spmd

    a = {k: np.asarray(v) for k, v in inputs.items()}

    def feature_major(g, n):
        return np.ascontiguousarray(g.reshape(n, P).T)

    def by_rows(w):
        return w.reshape(-1, P, w.shape[1]).transpose(1, 0, 2).reshape(P, -1)

    w = a["w_in"][0]
    at = np.cumsum([0, 512, 512, 1024, 1024, GRANK, 1024, 256, 256])
    gq, gk, gvw, grw, ga, sq, sk, svw = (w[:, at[i]:at[i + 1]] for i in range(8))
    order = [4 * (2 * (f // GROUP) + half) + f % GROUP for f in range(8) for half in range(2)]
    sq = sq.reshape(D, QH, HD)[:, order].reshape(D, D)
    swo = a["w_swa_out"][0].reshape(QH, HD, D)[order].reshape(D, D)
    bg, glo, wo, wq, pg = a["w_branch_gate"][0], a["w_gla_out"][0], a["w_out"][0], a["peer_wq"][0], a["w_ple_gate"][0]
    H = 512
    parts = {"gk": gk, "gv0": gvw[:, :H], "gv1": gvw[:, H:], "gq": gq, "gr0": grw[:, :H], "gr1": grw[:, H:],
             "kv": np.concatenate([sk, svw], 1), "sq0": sq[:, :H], "sq1": sq[:, H:]}
    for q in range(2):
        c = slice(q * H, q * H + H)
        parts.update({f"bgg{q}": bg[:, c], f"bgs{q}": bg[:, D + q * H:D + q * H + H], f"glo{q}": glo[:, c],
                      f"swo{q}": swo[:, c], f"wo{q}": wo[:, c], f"pg{q}": pg[:, c]})
    for q in range(4):
        parts[f"wq{q}"] = wq[:, q * H:q * H + H]
    slabs = np.zeros((len(FRONT_SLABS) + len(TAIL_SLABS), P, KT * SW), np.float32)
    for n, name in enumerate(FRONT_SLABS + TAIL_SLABS):
        if name == "pp":
            slabs[n, :, :2048] = by_rows(a["w_ple_proj"][0])
        else:
            slabs[n] = by_rows(parts[name])

    arrays = {
        "x": a["x"].reshape(SEQ, D), "slabs": slabs,
        "pT": a["p"].reshape(SEQ, 2, P).transpose(2, 1, 0),
        "g_mix": feature_major(a["norm_mix"][0], KT), "g_ple": feature_major(a["norm_ple"][0], KT),
        "g_on": feature_major(a["gla_onorm"][0], 2), "b_bg": feature_major(a["b_branch_gate"][0], 2 * KT),
        "sinks": a["swa_sinks"][0], "g_ffn": a["norm_ffn"][0], "g_fin": a["norm_final"],
        "wga": by_rows(ga).reshape(P, KT, GRANK),
        "wa2": np.concatenate([a["w_gla_a2"][0], a["b_gla_a"]], 0),
        "subk": a["peer_subkeys"][0].transpose(2, 0, 1),
        "u": a["peer_u"][0], "v": a["peer_v"][0], **shape_tables(),
    }
    arrays = {k: np.ascontiguousarray(v) for k, v in arrays.items()}
    nc = bacc.Bacc("TRN2", target_bir_lowering=False, num_devices=1)
    aps = {k: nc.dram_tensor(f"in_{k}", v.shape, F32, kind="ExternalInput").ap() for k, v in arrays.items()}
    out = nc.dram_tensor("out_0", (SEQ, D), F32, kind="ExternalOutput").ap()
    build(nc, aps, out)
    r = run_bass_kernel_spmd(nc, [{f"in_{k}": v for k, v in arrays.items()}], core_ids=[0])
    return r.results[0]["out_0"].reshape(1, SEQ, D)
```

```python
from contextlib import ExitStack

import numpy as np

import concourse.bass as bass
from concourse import mybir

ALU = mybir.AluOpType
ACT = mybir.ActivationFunctionType
AX = mybir.AxisListType
F32 = mybir.dt.float32
U32 = mybir.dt.uint32

P = 128
D = 1024
KT = D // P
SEQ = 1024
SEG = 256
NSEG = SEQ // SEG
TT = SEG // P
NTILE = SEQ // P
CHUNK = 64
EPS = 1e-6

GH, GDK, GDV, GRANK, GTEMP = 4, 128, 256, 16, 16.0
QH, KVH, HD = 16, 4, 64
GROUP = QH // KVH
BAND = 3 * CHUNK
FAR = 1e33

NH, NK, TOPK = 8, 128, 16
NHEAD = NTILE * NH
LOW = -3.0e38
SW = 512
RS = 2
US, VS, DS, CS = 4, 8, 4, 4
ODD = TOPK // 2
TK = 16

FRONT = [
    (0, []),
    (7, []),
    (7, [("gk", 2), ("gv0", 4)]),
    (4, [("gv1", 2), ("gq", 4)]),
    (4, [("gr0", 2), ("gr1", 4)]),
    (4, [("kv", 2)]),
    (2, [("sq0", 2)]),
    (6, [("sq1", 2), ("bgg0", 6)]),
    (4, [("glo0", 2), ("bgg1", 4)]),
    (8, [("glo1", 2)]),
    (8, [("bgs0", 2)]),
    (8, [("bgs1", 2)]),
    (10, [("swo0", 8), ("swo1", 10)]),
    (4, [("wo0", 2), ("wo1", 4)]),
    (0, []),
    (12, [("wq0", 6), ("wq1", 10)]),
    (8, [("wq2", 2), ("wq3", 6)]),
]
TAIL = [(0, []), (6, [("pg0", 3), ("pg1", 4), ("pp", 6)]), (0, [])]
SLABS = [w for _, ws in FRONT + TAIL for w, _ in ws]

LEAD = 18
FIRST, LAST = -LEAD, NHEAD + 6


def stages(n):
    s, j = divmod(n + LEAD, 16)
    found = []
    if j == 0 and 1 <= s <= NSEG:
        found.append(("front", s - 1, 16))
    if 0 <= s < NSEG:
        found.append(("front", s, j))
    i, j = divmod(n - 11, 8)
    if 0 <= i < NTILE and j < 3:
        found.append(("tail", i, j))
    return found


def table(kind):
    return FRONT if kind == "front" else TAIL


def uses_through(n):
    return sum(table(k)[j][0] for m in range(FIRST, n + 1) for k, _, j in stages(m))


def uses_at(kind, which, stage):
    total = 0
    for m in range(FIRST, LAST + 1):
        for item in stages(m):
            total += table(item[0])[item[2]][0]
            if item == (kind, which, stage):
                return total


def slab_reads():
    total, found = 0, []
    for n in range(FIRST, LAST + 1):
        for k, _, j in stages(n):
            found += [(w, n, total + u) for w, u in table(k)[j][1]]
            total += table(k)[j][0]
    return found


SLAB_READS = slab_reads()


class Count:

    def __init__(self):
        self.n = 0

    def next(self):
        self.n += 1
        return self.n


def build(nc, a, out):
    with ExitStack() as ctx:
        def sb(name, shape, dt=F32):
            return ctx.enter_context(nc.sbuf_tensor(name, shape, dt))

        def ps(name, shape):
            return ctx.enter_context(nc.psum_tensor(name, shape, F32))

        def sem(name):
            return ctx.enter_context(nc.semaphore(name))

        def dram(name, shape):
            return nc.dram_tensor(name, shape, F32, kind="Internal").ap()

        x1_d = dram("x1_d", (NTILE, P, D))
        h2_d = dram("h2_d", (NTILE, P, D))
        sc_d = dram("sc_d", (NTILE, P, NH * 2 * NK))

        ident = sb("ident", [P, P])
        tri = sb("tri", [P, P])
        chunk_of = sb("chunk_of", [P, 2])
        dist = sb("dist", [P, 2, BAND])
        iota16 = sb("iota16", [P, TOPK])
        g_mix = sb("g_mix", [P, KT])
        g_ple = sb("g_ple", [P, KT])
        g_on = sb("g_on", [P, 2])
        b_bg = sb("b_bg", [P, 2 * KT])
        sinks = sb("sinks", [P, QH])
        g_ffn = sb("g_ffn", [P, D])
        wga = sb("wga", [P, KT, GRANK])
        wa2 = sb("wa2", [GRANK + 1, GH * GDK])
        subk = sb("subk", [P, 2, NK])
        eps = sb("eps", [P, 1])

        slab = sb("slab", [P, RS, KT * SW])
        hT = sb("hT", [P, KT, SEG])
        rX = sb("rX", [P, 2048])
        rA = sb("rA", [P, 2048])
        rB = sb("rB", [P, 2048])
        rC = sb("rC", [P, 2048])
        rD = sb("rD", [P, 2048])
        rE = sb("rE", [P, 2048])
        xs = rX[:].rearrange("p (t n) -> p t n", t=TT)
        sl = rX[:, 0:2 * GROUP * BAND].rearrange("p (j n) -> p j n", n=BAND)
        gv = rA[:].rearrange("p (t n) -> p t n", t=TT)
        sqT = rA[:].rearrange("p (f n) -> p f n", f=8)
        ysw = rA[:]
        gr = rB[:].rearrange("p (t n) -> p t n", t=TT)
        yswT = rB[:].rearrange("p (f n) -> p f n", f=8)
        ysc = rB[:].rearrange("p (b t n) -> p b t n", b=2, t=TT)
        yglT = rC[:].rearrange("p (f n) -> p f n", f=8)
        h2 = rC[:].rearrange("p (t n) -> p t n", t=TT)
        gqT = rD[:, 0:1024].rearrange("p (h n) -> p h n", h=GH)
        kdec = rD[:, 1024:2048].rearrange("p (t n) -> p t n", t=TT)
        mT = rD[:].rearrange("p (f n) -> p f n", f=8)
        pq = rD[:].rearrange("p (b f n) -> p b f n", b=2, f=4)
        loga = rE[:, 0:1024].rearrange("p (t n) -> p t n", t=TT)
        zs = rE[:, 1024:2048].rearrange("p (t n) -> p t n", t=TT)
        gates = rE[:].rearrange("p (f n) -> p f n", f=8)
        tgate = rE[:, 0:1024]
        thT = rE[:, 1024:2048].rearrange("p (f n) -> p f n", f=8)
        g_fin = rE[:, 1024:2048]
        skT = sb("skT", [P, 2, CHUNK + SEG])
        sv = sb("sv", [P, TT + 1, KVH * HD])
        aT = sb("aT", [GRANK + 1, SEG])
        dec = sb("dec", [P, GH, 2 * TT])
        state = sb("state", [P, 2, GH, GDV])
        stat_x = sb("stat_x", [P, 3, TT])
        stat_h = sb("stat_h", [P, 3, TT])
        stat_t = sb("stat_t", [P, 3, 2])
        gstat = sb("gstat", [P, 3, GH])
        otok = sb("otok", [P, GH * GDV])
        ygl = otok[:]
        probs = sb("probs", [P, 2 * GROUP, 256])
        junk = probs[:, :, CHUNK:CHUNK + P]
        pT = sb("pT", [P, GROUP, 2, P])
        ths = pT[:].rearrange("p j b n -> p (j b n)")
        sm = sb("sm", [P, 5, 2 * GROUP])
        tX = sb("tX", [P, D])
        tpT = sb("tpT", [P, 2, P])

        ubuf = sb("ubuf", [P, US, D])
        vbuf = sb("vbuf", [P, VS, D])
        hbuf = sb("hbuf", [P, 2, D])
        acc = sb("acc", [P, D])
        diag = sb("diag", [P, DS, P])
        sct = sb("sct", [P, CS, 2, NK])
        vals = sb("vals", [P, 2, TOPK])
        lidx = sb("lidx", [P, 2, TOPK], U32)
        lidf = sb("lidf", [P, 2, TOPK])
        cand = sb("cand", [P, TOPK * TOPK])
        tv = sb("tv", [P, TOPK])
        negmax = sb("negmax", [P, 1])
        pos = sb("pos", [P, TOPK], U32)
        posi = sb("posi", [P, 2, TOPK], U32)
        posf = sb("posf", [P, 2, TOPK])
        hot = sb("hot", [P, 2, TOPK, TOPK])
        picked = sb("picked", [P, 2, TOPK])
        idx = sb("idx", [P, 2, TOPK], U32)
        gexp = sb("gexp", [P, 2, TOPK])
        gsum = sb("gsum", [P, 2, 1])
        ginv = sb("ginv", [P, 2, 1])
        dots = sb("dots", [P, 2, TOPK])
        gel = sb("gel", [P, 2, TOPK])
        wts = sb("wts", [P, 2, TOPK])

        bank = ps("bank", [P, 2, 512])
        wide = ps("wide", [P, 4, 512])
        ysum = ps("ysum", [P, 2, 512])

        const_in = sem("const_in")
        setup = sem("setup")
        x_in = sem("x_in")
        xres_in = sem("xres_in")
        slab_in = [sem(f"slab_in{i}") for i in range(RS)]
        bank_full = sem("bank_full")
        emptied = sem("emptied")
        vec_step = sem("vec_step")
        vec_done = sem("vec_done")
        squared = sem("squared")
        root_done = sem("root_done")
        rstd_done = sem("rstd_done")
        scaled = sem("scaled")
        tail_scaled = sem("tail_scaled")
        gate_step = sem("gate_step")
        u_full = sem("u_full")
        o_full = sem("o_full")
        logit_full = sem("logit_full")
        window_exp = sem("window_exp")
        x1_out = sem("x1_out")
        h2_out = sem("h2_out")
        sc_out = [sem("sc_out0"), sem("sc_out1")]
        score_in = [sem(f"score_in{i}") for i in range(CS)]
        h_in = sem("h_in")
        acc_in = sem("acc_in")
        topk_step = sem("topk_step")
        topk_exp = sem("topk_exp")
        idx_ready = sem("idx_ready")
        held = sem("held")
        u_in = [sem(f"u_in{i}") for i in range(US)]
        v_in = [sem(f"v_in{i}") for i in range(VS)]
        u_used = sem("u_used")
        v_used_dve = sem("v_used_dve")
        v_used_pe = sem("v_used_pe")
        gelu_done = sem("gelu_done")
        wts_step = sem("wts_step")
        diag_done = sem("diag_done")
        x2_done = sem("x2_done")
        tp_in = sem("tp_in")
        gfin_in = sem("gfin_in")
        tail_out = sem("tail_out")

        consts = [(ident[:], a["ident"]), (tri[:], a["tri"]), (chunk_of[:], a["chunk_of"]),
                  (dist[:], a["dist"]), (iota16[:], a["iota16"].partition_broadcast(P)),
                  (g_mix[:], a["g_mix"]), (g_ple[:], a["g_ple"]), (g_on[:], a["g_on"]),
                  (b_bg[:], a["b_bg"]), (sinks[:], a["sinks"].partition_broadcast(P)),
                  (g_ffn[:], a["g_ffn"].partition_broadcast(P)), (wga[:], a["wga"]),
                  (wa2[:], a["wa2"]), (subk[:], a["subk"])]
        CONST_READY = 16 * len(consts)
        SETUP = 6

        x_t = a["x"].rearrange("(t p) d -> p t d", p=P)
        out_t = out.rearrange("(t p) d -> t p d", p=P)
        uw = [wide[:, 2 * b:2 * b + 2, :].rearrange("p b (h n) -> p (b h) n", h=2) for b in range(2)]
        ow = uw[0]

        def done_before(n):
            return n - FIRST

        block = ctx.enter_context(nc.Block())

        @block.sync
        def _(sp):
            def tiles(t, s):
                return t[TT * s:TT * s + TT].rearrange("t p d -> p t d")

            def front(s, j):
                if j == 12:
                    sp.wait_ge(window_exp, WEXP * (4 * s + 4))
                    sp.dma_start(xs, x_t[:, TT * s:TT * s + TT, :]).then_inc(xres_in, 16)
                if j == 15:
                    sp.wait_ge(vec_done, done_before(16 * s - LEAD + 15))
                    sp.dma_start(tiles(x1_d, s), xs).then_inc(x1_out, 16)
                    sp.dma_start(tiles(h2_d, s), h2).then_inc(h2_out, 16)
                    if s + 1 < NSEG:
                        sp.wait_ge(x1_out, 16 * (s + 1))
                        sp.dma_start(xs, x_t[:, TT * s + TT:TT * s + 2 * TT, :]).then_inc(x_in, 16)

            def scores_out(s, stage):
                for b in range(2):
                    q = 2 * (stage - 15) + b
                    sp.wait_ge(emptied, uses_at("front", s, stage) - (4 if b == 0 else 0))
                    sp.dma_start(tiles(sc_d, s)[:, :, q * 512:q * 512 + 512], ysc[:, b]).then_inc(sc_out[b], 16)

            loaded = Count()

            def slabs_for(n):
                for m, (name, slot, _) in enumerate(SLAB_READS):
                    if slot == n:
                        if m >= RS:
                            sp.wait_ge(bank_full, SLAB_READS[m - RS][2])
                        w = 2 * D if name == "pp" else KT * SW
                        sp.dma_start(slab[:, m % RS, 0:w], a["slabs"][SLABS.index(name), :, 0:w]
                                     ).then_inc(slab_in[m % RS], 16)
                        loaded.next()

            sp.dma_start(xs, x_t[:, 0:TT, :]).then_inc(x_in, 16)
            for dst, src in consts:
                sp.dma_start(dst, src).then_inc(const_in, 16)
            for n in range(FIRST, LAST + 1):
                before = stages(n - 1)
                for s in range(NSEG):
                    if ("front", s, 15) in before:
                        scores_out(s, 15)
                    if ("front", s, 16) in before:
                        scores_out(s, 16)
                m = n + 2
                if 0 <= m < NHEAD:
                    i, h = divmod(m, NH)
                    if m % 16 == 0:
                        for b in range(2):
                            sp.wait_ge(sc_out[b], 32 * (m // 16) + 16)
                    if m % 16 == 4:
                        for b in range(2):
                            sp.wait_ge(sc_out[b], 32 * (m // 16) + 32)
                    if m >= CS:
                        sp.wait_ge(topk_step, TK * (m - CS + 1))
                    sp.dma_start(sct[:, m % CS], sc_d[i, :, h * 256:h * 256 + 256].rearrange("p (q n) -> p q n", q=2)
                                 ).then_inc(score_in[m % CS], 16)
                i, h = divmod(n + 1, NH)
                if h == 0 and 0 <= i < NTILE:
                    sp.wait_ge(h2_out, 16 * (i // TT + 1))
                    if i >= 2:
                        sp.wait_ge(u_used, US + (i - 1) * NH * TOPK)
                    sp.dma_start(hbuf[:, i % 2, :], h2_d[i]).then_inc(h_in, 16)
                i, h = divmod(n, NH)
                if h == 0 and 0 <= i <= NTILE:
                    if i:
                        sp.wait_ge(x2_done, i)
                        sp.dma_start(tpT[:], a["pT"][:, :, (i - 1) * P:i * P]).then_inc(tp_in, 16)
                    if i < NTILE:
                        sp.wait_ge(x1_out, 16 * (i // TT + 1))
                        sp.dma_start(acc[:], x1_d[i]).then_inc(acc_in, 16)
                for kind, i, j in before:
                    if kind == "tail" and j == 1:
                        sp.wait_ge(bank_full, uses_at("tail", i, 1))
                        sp.dma_start(g_fin, a["g_fin"].partition_broadcast(P)).then_inc(gfin_in, 16)
                for kind, i, j in stages(n - 2):
                    if kind == "tail" and j == 2:
                        sp.wait_ge(vec_done, done_before(n - 1))
                        sp.dma_start(out_t[i], tX[:]).then_inc(tail_out, 16)
                for kind, s, j in stages(n):
                    if kind == "front":
                        front(s, j)
                slabs_for(n + 1)
            assert loaded.n == len(SLAB_READS)
            sp.wait_ge(vec_done, done_before(LAST))
            sp.dma_start(out_t[NTILE - 1], tX[:]).then_inc(tail_out, 16)
            sp.wait_ge(tail_out, 16 * NTILE)

        @block.gpsimd
        def _(pool):
            def hold(s, value):
                pool.wait_ge(s, value)
                pool.sem_inc(held, 1)

            def gather(rows, dst, b, k, done):
                nc.gpsimd.indirect_dma_start(
                    out=dst, out_offset=None, in_=rows,
                    in_offset=bass.IndirectOffsetOnAxis(ap=idx[:, b, k:k + 1], axis=0)).then_inc(done, 16)

            with nc.gpsimd.Fori(0, NHEAD // 2) as i:
                for b in range(2):
                    hold(idx_ready, i * 2 + b + 1)
                    for k in range(TOPK):
                        hold(u_used, i * (2 * TOPK) + b * TOPK + k + 1)
                        gather(a["u"], ubuf[:, k % US, :], b, k, u_in[k % US])
                    for k in range(TOPK):
                        hold(v_used_pe if k % 2 else v_used_dve, i * TOPK + b * ODD + k // 2 + 1)
                        gather(a["v"], vbuf[:, k % VS, :], b, k, v_in[k % VS])

        @block.tensor
        def _(pe):
            mm = nc.tensor.matmul
            used = Count()
            slabs = Count()

            def bank_for():
                n = used.next() - 1
                if n >= 2:
                    pe.wait_ge(emptied, n - 1)
                return bank[:, n % 2, :]

            def all_emptied():
                pe.wait_ge(emptied, used.n)

            def after_vector(n):
                pe.wait_ge(vec_done, done_before(n))

            def next_slab():
                n = slabs.next() - 1
                pe.wait_ge(slab_in[n % RS], 16 * (n // RS + 1))
                return slab[:, n % RS, :].rearrange("p (k n) -> p k n", k=KT)

            def turned(src):
                for f in range(0, KT, 2):
                    b = bank_for()
                    for g in range(2):
                        for t in range(TT):
                            c0 = g * SEG + t * P
                            m = nc.tensor.transpose(b[:, c0:c0 + P], src[:, t, (f + g) * P:(f + g) * P + P], ident[:])
                    m.then_inc(bank_full, 1)

            def by_feature(w, tiles, src):
                for f in range(0, tiles, 2):
                    b = bank_for()
                    for g in range(2):
                        for k in range(KT):
                            m = mm(b[:, g * SEG:g * SEG + SEG], w[:, k, (f + g) * P:(f + g) * P + P], src[:, k, :],
                                   start=(k == 0), stop=(k == KT - 1))
                    m.then_inc(bank_full, 1)

            def by_token(w, src):
                for t in range(TT):
                    b = bank_for()
                    for k in range(KT):
                        m = mm(b, src[:, k, t * P:t * P + P], w[:, k, :], start=(k == 0), stop=(k == KT - 1))
                    m.then_inc(bank_full, 1)

            def u_of(t):
                for half in range(2):
                    r0 = half * CHUNK
                    for h in range(GH):
                        m = mm(uw[half][:, h, :], kdec[r0:r0 + CHUNK, t, h * GDK:h * GDK + GDK],
                               gv[r0:r0 + CHUNK, t, h * GDV:h * GDV + GDV], start=True, stop=True)
                    m.then_inc(u_full, 1)

            def o_of(t):
                for half in range(2):
                    r0 = half * CHUNK
                    c0 = t * P + r0
                    for h in range(GH):
                        m = mm(ow[r0:r0 + CHUNK, h, :], gqT[:, h, c0:c0 + CHUNK], state[:, half, h, :],
                               start=True, stop=True)
                m.then_inc(o_full, 1)

            def turn_o():
                for odd in range(2):
                    b = bank_for()
                    for j in range(4):
                        f = 2 * j + odd
                        m = nc.tensor.transpose(b[:, j * P:j * P + P], otok[:, f * P:f * P + P], ident[:])
                    m.then_inc(bank_full, 1)

            def logits(batch):
                t = batch // 2
                for e in range(2):
                    g = 2 * (batch % 2) + e
                    r0 = (g % 2) * HD
                    for j in range(GROUP):
                        o = wide[:, 2 * e + j // 2, (j % 2) * BAND:(j % 2) * BAND + BAND]
                        m = mm(o, sqT[r0:r0 + HD, (g // 2) * GROUP + j, t * P:t * P + P],
                               skT[r0:r0 + HD, g // 2, t * P:t * P + BAND], start=True, stop=True)
                m.then_inc(logit_full, 1)

            def values(batch):
                t = batch // 2
                for e in range(2):
                    g = 2 * (batch % 2) + e
                    r0 = (g % 2) * HD
                    for half in range(2):
                        b = bank_for()
                        for j in range(2):
                            for blk in range(2):
                                c0 = (2 * j + blk) * P
                                m = nc.tensor.transpose(b[:, c0:c0 + P], probs[:, GROUP * e + 2 * half + j,
                                                                              blk * P:blk * P + P], ident[:])
                        m.then_inc(bank_full, 1)
                    all_emptied()
                    b = bank_for()
                    for blk in range(2):
                        m = mm(b[r0:r0 + HD, :], sv[:, t + blk, g * HD:g * HD + HD], pT[:, :, blk, :],
                               start=(blk == 0), stop=(blk == 1))
                    m.then_inc(bank_full, 1)

            def front(n, s, j):
                if j == 1:
                    pe.wait_ge(scaled, TT * (s + 1))
                    turned(xs)
                    all_emptied()
                    b = bank_for()
                    for k in range(KT):
                        m = mm(b[0:GRANK, 0:SEG], wga[:, k, :], hT[:, k, :], start=(k == 0), stop=(k == KT - 1))
                    m.then_inc(bank_full, 1)
                    all_emptied()
                    for t in range(TT):
                        mm(bank_for(), aT[:, t * P:t * P + P], wa2[:], start=True, stop=True).then_inc(bank_full, 1)
                elif j == 2:
                    by_token(next_slab(), hT)
                    by_token(next_slab(), hT)
                    after_vector(n)
                    b = bank_for()
                    for t in range(TT):
                        for h in range(GH):
                            c0 = h * 2 * TT + 2 * t
                            m = mm(b[:, c0:c0 + 2], loga[:, t, h * GDK:h * GDK + GDK], chunk_of[:],
                                   start=True, stop=True)
                    m.then_inc(bank_full, 1)
                    for t in range(TT):
                        mm(bank_for(), tri[:], loga[:, t, :], start=True, stop=True).then_inc(bank_full, 1)
                elif j == 3:
                    by_token(next_slab(), hT)
                    by_feature(next_slab(), 4, hT)
                    all_emptied()
                    after_vector(n)
                    u_of(0)
                elif j == 4:
                    by_token(next_slab(), hT)
                    by_token(next_slab(), hT)
                    after_vector(n)
                    o_of(0)
                elif j == 5:
                    w = next_slab()
                    by_feature(w, 2, hT)
                    b = bank_for()
                    for t in range(TT):
                        for k in range(KT):
                            m = mm(b[:, t * 256:t * 256 + 256], hT[:, k, t * P:t * P + P], w[:, k, 256:512],
                                   start=(k == 0), stop=(k == KT - 1))
                    m.then_inc(bank_full, 1)
                    after_vector(n)
                    turn_o()
                    u_of(1)
                elif j == 6:
                    by_feature(next_slab(), 4, hT)
                    after_vector(n)
                    o_of(1)
                elif j == 7:
                    by_feature(next_slab(), 4, hT)
                    after_vector(n)
                    turn_o()
                    by_feature(next_slab(), 4, hT)
                    pe.wait_ge(emptied, used.n - 2)
                    logits(0)
                elif j == 8:
                    by_feature(next_slab(), 4, yglT)
                    by_feature(next_slab(), 4, hT)
                    after_vector(n)
                    logits(1)
                elif j in (9, 10, 11):
                    by_feature(next_slab(), 4, yglT if j == 9 else hT)
                    after_vector(n)
                    if j < 11:
                        logits(j - 7)
                    values(j - 9)
                elif j == 12:
                    after_vector(n)
                    values(3)
                    all_emptied()
                    by_feature(next_slab(), 4, yswT)
                    by_feature(next_slab(), 4, yswT)
                elif j == 13:
                    after_vector(n)
                    by_token(next_slab(), mT)
                    by_token(next_slab(), mT)
                elif j in (15, 16):
                    if j == 15:
                        after_vector(n)
                        turned(h2)
                        all_emptied()
                    for b2 in range(2):
                        by_feature(next_slab(), 4, hT)
                        all_emptied()
                        for t in range(TT):
                            b = bank_for()
                            for f in range(4):
                                m = mm(b[:, f * P:f * P + P], pq[:, b2, f, t * P:t * P + P], subk[:, f % 2, :],
                                       start=True, stop=True)
                            m.then_inc(bank_full, 1)

            def tail(n, i, j):
                if j != 1:
                    return
                pe.wait_ge(tail_scaled, i + 1)
                for f in range(0, KT, 4):
                    b = bank_for()
                    for g in range(4):
                        m = nc.tensor.transpose(b[:, g * P:g * P + P], ths[:, (f + g) * P:(f + g) * P + P], ident[:])
                    m.then_inc(bank_full, 1)
                all_emptied()
                for q in range(2):
                    w = next_slab()
                    b = bank_for()
                    for k in range(KT):
                        m = mm(b, thT[:, k, :], w[:, k, :], start=(k == 0), stop=(k == KT - 1))
                    m.then_inc(bank_full, 1)
                w = next_slab().rearrange("p k n -> p (k n)")[:, 0:2048].rearrange("p (k n) -> p k n", k=2)
                pe.wait_ge(tp_in, 16 * (i + 1))
                for q in range(2):
                    b = bank_for()
                    for k in range(2):
                        m = mm(b, tpT[:, k, :], w[:, k, q * 512:q * 512 + 512], start=(k == 0), stop=(k == 1))
                    m.then_inc(bank_full, 1)

            def peer_head(n):
                i, h = divmod(n, NH)
                if h == 0 and i:
                    pe.wait_ge(x2_done, i)
                for kk in range(ODD):
                    k = 2 * kk + 1
                    m0 = n * ODD + kk
                    pe.wait_ge(diag_done, m0 + 1)
                    pe.wait_ge(v_in[k % VS], (n * (TOPK // VS) + k // VS + 1) * 16)
                    for c in range(2):
                        m = mm(ysum[:, c, :], diag[:, m0 % DS, :], vbuf[:, k % VS, c * 512:c * 512 + 512],
                               start=(h == 0 and kk == 0), stop=(h == NH - 1 and kk == ODD - 1))
                    m.then_inc(v_used_pe, 1)

            pe.wait_ge(const_in, CONST_READY)
            pe.wait_ge(setup, SETUP)
            for n in range(FIRST, LAST + 1):
                if 0 <= n < NHEAD:
                    peer_head(n)
                for kind, s, j in stages(n):
                    (front if kind == "front" else tail)(n, s, j)
                assert used.n == uses_through(n)

        @block.scalar
        def _(act):
            fn = nc.scalar.activation
            used = Count()
            squares = Count()
            roots = Count()
            gate_ops = Count()
            exps = Count()

            def full():
                n = used.next()
                act.wait_ge(bank_full, n)
                return bank[:, (n - 1) % 2, :]

            def after_vector(n):
                act.wait_ge(vec_done, done_before(n))

            def copied(dst, src, **kw):
                fn(dst, src, kw.pop("func", ACT.Copy), **kw).then_inc(emptied, 1)

            def square_sums(pieces):
                for src, dst in pieces:
                    if squares.n:
                        act.wait_ge(squared, squares.n)
                    squares.next()
                    fn(junk[:, 0:src.shape[-1] // P, :], src.rearrange("p (j n) -> p j n", n=P), ACT.Square,
                       accum_out=dst).then_inc(squared, 1)
                act.wait_ge(squared, squares.n)

            def root(dst, src, width):
                roots.next()
                fn(dst, src, ACT.Sqrt, bias=eps[:], scale=1.0 / width).then_inc(root_done, 1)

            def window_exps():
                for j in range(2 * GROUP):
                    exps.next()
                    fn(probs[:, j, CHUNK:256], sl[:, j, :], ACT.Exp, bias=sm[:, 1, j:j + 1],
                       accum_out=sm[:, 3, j:j + 1]).then_inc(window_exp, 1)
                exps.next()
                fn(sm[:, 4, :], sm[:, 2, :], ACT.Exp).then_inc(window_exp, 1)

            def sigmoids(f0, b0):
                for f in range(0, 4, 2):
                    b = full()
                    for g in range(2):
                        m = fn(gates[:, f0 + f + g, :], b[:, g * SEG:g * SEG + SEG], ACT.Sigmoid,
                               bias=b_bg[:, b0 + f + g:b0 + f + g + 1])
                    m.then_inc(emptied, 1)

            def window_out(batch):
                t = batch // 2
                for e in range(2):
                    g = 2 * (batch % 2) + e
                    r0 = (g % 2) * HD
                    for half in range(2):
                        copied(pT[:, 2 * half:2 * half + 2, :, :].rearrange("p j b n -> p (j b n)"), full())
                    copied(yswT[r0:r0 + HD, (g // 2) * GROUP:(g // 2) * GROUP + GROUP, t * P:t * P + P],
                           full()[r0:r0 + HD, :].rearrange("p (j n) -> p j n", j=GROUP))

            def turn_o(t):
                for odd in range(2):
                    copied(yglT[:, odd:8:2, t * P:t * P + P], full().rearrange("p (f n) -> p f n", f=4),
                           scale=g_on[:, odd:odd + 1])

            def o_stats():
                square_sums([(ow[:, h, :], gstat[:, 0, h:h + 1]) for h in range(GH)])
                root(gstat[:, 1, :], gstat[:, 0, :], GDV)

            def front(n, s, j):
                if j == 0:
                    act.wait_ge(x_in, 16 * (s + 1))
                    if n > FIRST:
                        after_vector(n)
                    square_sums([(xs[:, t, :], stat_x[:, 0, t:t + 1]) for t in range(TT)])
                    root(stat_x[:, 1, :], stat_x[:, 0, :], D)
                elif j == 1:
                    after_vector(n)
                    for t in range(TT):
                        fn(xs[:, t, :], xs[:, t, :], ACT.Copy, scale=stat_x[:, 2, t:t + 1]).then_inc(scaled, 1)
                    for f in range(0, KT, 2):
                        b = full()
                        for g in range(2):
                            m = fn(hT[:, f + g, :], b[:, g * SEG:g * SEG + SEG], ACT.Copy, scale=g_mix[:, f + g:f + g + 1])
                        m.then_inc(emptied, 1)
                    copied(aT[0:GRANK, :], full()[0:GRANK, 0:SEG])
                    for t in range(TT):
                        b = full()
                        fn(zs[:, t, :], b, ACT.Copy)
                        copied(loga[:, t, :], b, func=ACT.Abs)
                    act.wait_ge(emptied, used.n)
                    gate_ops.next()
                    fn(loga, loga, ACT.Exp, scale=-1.0).then_inc(gate_step, 1)
                    act.wait_ge(gate_step, gate_ops.n)
                    gate_ops.next()
                    fn(loga, loga, ACT.Ln, bias=1.0).then_inc(gate_step, 1)
                elif j == 2:
                    for t in range(TT):
                        copied(kdec[:, t, :], full())
                    for t in range(TT):
                        copied(gv[:, t, 0:512], full())
                    copied(dec[:].rearrange("p h c -> p (h c)"), full()[:, 0:GH * 2 * TT], func=ACT.Exp, scale=1.0 / GTEMP)
                    for t in range(TT):
                        copied(loga[:, t, :], full(), func=ACT.Exp, scale=1.0 / GTEMP)
                elif j == 3:
                    for t in range(TT):
                        copied(gv[:, t, 512:1024], full())
                    for h in range(0, GH, 2):
                        copied(gqT[:, h:h + 2, :].rearrange("p h n -> p (h n)"), full(), scale=GDK ** -0.5)
                elif j == 4:
                    if s:
                        for b in range(2):
                            act.wait_ge(sc_out[b], 32 * s)
                    for half in range(2):
                        for t in range(TT):
                            copied(gr[:, t, half * 512:half * 512 + 512], full(), func=ACT.Silu)
                    act.wait_ge(o_full, TT * s + 1)
                    o_stats()
                elif j == 5:
                    copied(skT[:, :, CHUNK:], full().rearrange("p (f n) -> p f n", f=2))
                    copied(sv[:, 1:TT + 1, :], full().rearrange("p (t n) -> p t n", t=TT))
                    if s:
                        act.wait_ge(h2_out, 16 * s)
                    turn_o(0)
                elif j == 6:
                    for f in range(0, 4, 2):
                        copied(sqT[:, f:f + 2, :].rearrange("p f n -> p (f n)"), full(), scale=HD ** -0.5)
                    act.wait_ge(o_full, TT * s + 2)
                    o_stats()
                elif j == 7:
                    for f in range(4, 8, 2):
                        copied(sqT[:, f:f + 2, :].rearrange("p f n -> p (f n)"), full(), scale=HD ** -0.5)
                    turn_o(1)
                    after_vector(n)
                    sigmoids(0, 0)
                elif j == 8:
                    for q in range(2):
                        copied(ygl[:, q * 512:q * 512 + 512], full())
                    after_vector(n)
                    sigmoids(4, 4)
                    window_exps()
                elif j in (9, 10, 11):
                    after_vector(n)
                    if j == 9:
                        for q in range(2):
                            copied(ygl[:, q * 512:q * 512 + 512], full())
                    elif j == 10:
                        sigmoids(0, 8)
                    else:
                        sigmoids(4, 12)
                    window_out(j - 9)
                    window_exps()
                elif j == 12:
                    after_vector(n)
                    window_out(3)
                    for q in range(4):
                        copied(ysw[:, q * 512:q * 512 + 512], full())
                elif j == 13:
                    after_vector(n)
                    for q in range(2):
                        for t in range(TT):
                            copied(h2[:, t, q * 512:q * 512 + 512], full())
                elif j == 14:
                    after_vector(n)
                    root(stat_h[:, 1, :], stat_h[:, 0, :], D)
                else:
                    after_vector(n)
                    if j == 15:
                        for f in range(0, KT, 2):
                            copied(hT[:, f:f + 2, :].rearrange("p f n -> p (f n)"), full())
                    for b2 in range(2):
                        for f in range(0, 4, 2):
                            copied(pq[:, b2, f:f + 2, :].rearrange("p f n -> p (f n)"), full())
                        if j == 16:
                            act.wait_ge(sc_out[b2], 32 * s + 16)
                        for t in range(TT):
                            copied(ysc[:, b2, t, :], full())

            def tail(n, i, j):
                after_vector(n)
                if j == 0:
                    act.wait_ge(x2_done, i + 1)
                    square_sums([(tX[:], stat_t[:, 0, 0:1])])
                    root(stat_t[:, 1, 0:1], stat_t[:, 0, 0:1], D)
                elif j == 1:
                    fn(ths, tX[:], ACT.Copy, scale=stat_t[:, 2, 0:1]).then_inc(tail_scaled, 1)
                    for f in range(0, KT, 4):
                        b = full()
                        for g in range(4):
                            m = fn(thT[:, f + g, :], b[:, g * P:g * P + P], ACT.Copy, scale=g_ple[:, f + g:f + g + 1])
                        m.then_inc(emptied, 1)
                    for q in range(2):
                        copied(tgate[:, q * 512:q * 512 + 512], full(), func=ACT.Sigmoid)
                    for q in range(2):
                        copied(ths[:, q * 512:q * 512 + 512], full())
                else:
                    root(stat_t[:, 1, 1:2], stat_t[:, 0, 1:2], D)

            def peer_exp(m):
                act.wait_ge(topk_step, TK * m + 11)
                if m >= 2:
                    act.wait_ge(wts_step, 2 * (m - 1))
                fn(gexp[:, m % 2, :], tv[:], ACT.Exp, bias=negmax[:], accum_out=gsum[:, m % 2, :]).then_inc(topk_exp, 1)

            def peer_head(n):
                act.wait_ge(u_used, US + (n + 1) * TOPK)
                if n >= 2:
                    act.wait_ge(wts_step, 2 * (n - 1))
                fn(gel[:, n % 2, :], dots[:, n % 2, :], ACT.Gelu_apprx_tanh).then_inc(gelu_done, 1)
                act.wait_ge(wts_step, 2 * (n + 1))
                for kk in range(ODD):
                    m0 = n * ODD + kk
                    if m0 >= DS:
                        act.wait_ge(v_used_pe, VS // 2 + m0 - DS + 1)
                    fn(diag[:, m0 % DS, :], ident[:], ACT.Copy,
                       scale=wts[:, n % 2, 2 * kk + 1:2 * kk + 2]).then_inc(diag_done, 1)

            act.wait_ge(const_in, CONST_READY)
            act.wait_ge(setup, SETUP)
            for n in range(FIRST, LAST + 1):
                if 0 <= n + 1 < NHEAD:
                    peer_exp(n + 1)
                if 0 <= n < NHEAD:
                    peer_head(n)
                for kind, s, j in stages(n):
                    (front if kind == "front" else tail)(n, s, j)
                assert used.n == uses_through(n)

        @block.vector
        def _(dve):
            v = nc.vector
            steps = Count()
            roots = Count()

            def step(ins):
                steps.next()
                ins.then_inc(vec_step, 1)

            def settle():
                if steps.n:
                    dve.wait_ge(vec_step, steps.n)

            def inverse(dst, src):
                dve.wait_ge(root_done, roots.next())
                step(v.reciprocal(dst, src))

            def states(s, t):
                for half in range(2):
                    settle()
                    dve.wait_ge(u_full, 2 * TT * s + 2 * t + half + 1)
                    for h in range(GH):
                        step(v.scalar_tensor_tensor(
                            out=state[:, half, h, :], in0=state[:, 1 - half, h, :],
                            scalar=dec[:, h, 2 * t + half:2 * t + half + 1], in1=uw[half][:, h, :],
                            op0=ALU.mult, op1=ALU.add))

            def gated_o(t):
                inverse(gstat[:, 2, :], gstat[:, 1, :])
                settle()
                for h in range(GH):
                    step(v.scalar_tensor_tensor(
                        out=otok[:, h * GDV:h * GDV + GDV], in0=ow[:, h, :], scalar=gstat[:, 2, h:h + 1],
                        in1=gr[:, t, h * GDV:h * GDV + GDV], op0=ALU.mult, op1=ALU.mult))

            def biased(s, batch):
                dve.wait_ge(logit_full, 4 * s + batch + 1)
                first = s == 0 and batch < 2
                hd0 = (batch % 2) * 2 * GROUP
                for j in range(2 * GROUP):
                    slope = 2.0 ** (-8.0 * (hd0 + j + 1) / QH)
                    step(v.scalar_tensor_tensor(
                        out=sl[:, j, :], in0=dist[:, 0 if first else 1, :], scalar=-slope,
                        in1=wide[:, j // 2, (j % 2) * BAND:(j % 2) * BAND + BAND], op0=ALU.mult, op1=ALU.add))
                settle()
                step(v.tensor_reduce(sm[:, 0, :], sl, AX.X, ALU.max))
                settle()
                step(v.tensor_tensor(sm[:, 0, :], sm[:, 0, :], sinks[:, hd0:hd0 + 2 * GROUP], ALU.max))
                settle()
                step(v.tensor_tensor(sm[:, 2, :], sinks[:, hd0:hd0 + 2 * GROUP], sm[:, 0, :], ALU.subtract))
                step(v.tensor_scalar(sm[:, 1, :], sm[:, 0, :], -1.0, None, ALU.mult))

            def normed_probs(s, batch):
                dve.wait_ge(window_exp, WEXP * (4 * s + batch + 1))
                step(v.tensor_tensor(sm[:, 3, :], sm[:, 3, :], sm[:, 4, :], ALU.add))
                settle()
                step(v.reciprocal(sm[:, 4, :], sm[:, 3, :]))
                settle()
                step(v.tensor_tensor(probs[:, :, CHUNK:256], probs[:, :, CHUNK:256],
                                     sm[:, 4, :].unsqueeze(2).broadcast_to([P, 2 * GROUP, BAND]), ALU.mult))

            def front(s, j):
                if j == 0:
                    inverse(stat_x[:, 2, :], stat_x[:, 1, :])
                elif j == 1:
                    dve.wait_ge(gate_step, 2 * (s + 1))
                    step(v.scalar_tensor_tensor(out=loga, in0=zs, scalar=0.0, in1=loga, op0=ALU.min, op1=ALU.subtract))
                elif j == 2:
                    step(v.tensor_tensor(kdec, kdec, loga, ALU.mult))
                elif j == 3:
                    states(s, 0)
                elif j == 4:
                    gated_o(0)
                elif j == 5:
                    states(s, 1)
                elif j == 6:
                    gated_o(1)
                elif j == 7:
                    biased(s, 0)
                elif j in (8, 9, 10):
                    normed_probs(s, j - 8)
                    biased(s, j - 7)
                    if j < 10:
                        q = j - 8
                        step(v.tensor_tensor(rD[:, q * 1024:q * 1024 + 1024], rE[:, q * 1024:q * 1024 + 1024], ygl, ALU.mult))
                elif j == 11:
                    normed_probs(s, 3)
                elif j == 12:
                    step(v.tensor_tensor(ysw, ysw, rE[:], ALU.mult))
                    if s + 1 < NSEG:
                        step(v.tensor_copy(skT[:, :, 0:CHUNK], skT[:, :, SEG:SEG + CHUNK]))
                        step(v.tensor_copy(sv[:, 0, :], sv[:, TT, :]))
                    settle()
                    step(v.tensor_tensor(rD[:], rD[:], ysw, ALU.add))
                elif j == 13:
                    dve.wait_ge(xres_in, 16 * (s + 1))
                    step(v.tensor_tensor(rX[:], rX[:], rC[:], ALU.add))
                    settle()
                    for t in range(TT):
                        step(v.scalar_tensor_tensor(out=h2[:, t, :], in0=xs[:, t, :], scalar=1.0, in1=xs[:, t, :],
                                                    op0=ALU.mult, op1=ALU.mult, accum_out=stat_h[:, 0, t:t + 1]))
                elif j == 14:
                    inverse(stat_h[:, 2, :], stat_h[:, 1, :])
                    settle()
                    for t in range(TT):
                        step(v.scalar_tensor_tensor(out=h2[:, t, :], in0=xs[:, t, :], scalar=stat_h[:, 2, t:t + 1],
                                                    in1=g_ffn[:], op0=ALU.mult, op1=ALU.mult))

            def tail(i, j):
                if j == 0:
                    inverse(stat_t[:, 2, 0:1], stat_t[:, 1, 0:1])
                elif j == 1:
                    step(v.tensor_tensor(ths, ths, tgate, ALU.mult))
                    settle()
                    step(v.tensor_tensor(tX[:], tX[:], ths, ALU.add))
                    settle()
                    step(v.scalar_tensor_tensor(out=ths, in0=tX[:], scalar=1.0, in1=tX[:], op0=ALU.mult, op1=ALU.mult,
                                                accum_out=stat_t[:, 0, 1:2]))
                else:
                    inverse(stat_t[:, 2, 1:2], stat_t[:, 1, 1:2])
                    settle()
                    dve.wait_ge(gfin_in, 16 * (i + 1))
                    step(v.scalar_tensor_tensor(out=tX[:], in0=tX[:], scalar=stat_t[:, 2, 1:2], in1=g_fin,
                                                op0=ALU.mult, op1=ALU.mult))

            def stage_parts(n):
                dve.wait_ge(emptied, uses_through(n)) if uses_through(n) else None
                for kind, s, j in stages(n):
                    (front if kind == "front" else tail)(s, j)
                settle()
                dve.sem_inc(vec_done, 1)

            def topk(m, j):
                base = TK * m
                row = sct[:, m % CS]
                if base + j:
                    dve.wait_ge(topk_step, base + j)
                if j == 0:
                    dve.wait_ge(score_in[m % CS], 16 * (m // CS + 1))
                    for q in range(2):
                        ins = v.max(vals[:, q, 0:8], row[:, q, :])
                elif j == 1:
                    for q in range(2):
                        ins = v.max_index(lidx[:, q, 0:8], vals[:, q, 0:8], row[:, q, :])
                elif j == 2:
                    for q in range(2):
                        ins = v.match_replace(row[:, q, :], vals[:, q, 0:8], row[:, q, :], LOW)
                elif j == 3:
                    for q in range(2):
                        ins = v.max(vals[:, q, 8:16], row[:, q, :])
                elif j == 4:
                    for q in range(2):
                        ins = v.max_index(lidx[:, q, 8:16], vals[:, q, 8:16], row[:, q, :])
                elif j == 5:
                    ins = v.tensor_tensor(cand[:].rearrange("p (i j) -> p i j", i=TOPK),
                                          vals[:, 0, :].unsqueeze(2).broadcast_to([P, TOPK, TOPK]),
                                          vals[:, 1, :].unsqueeze(1).broadcast_to([P, TOPK, TOPK]), ALU.add)
                elif j == 6:
                    if m:
                        dve.wait_ge(topk_exp, m)
                    ins = v.max(tv[:, 0:8], cand[:])
                elif j == 7:
                    ins = v.max_index(pos[:, 0:8], tv[:, 0:8], cand[:])
                elif j == 8:
                    ins = v.match_replace(cand[:], tv[:, 0:8], cand[:], LOW)
                elif j == 9:
                    ins = v.max(tv[:, 8:16], cand[:])
                elif j == 10:
                    v.max_index(pos[:, 8:16], tv[:, 8:16], cand[:])
                    ins = v.tensor_scalar(negmax[:], tv[:, 0:1], -1.0, None, ALU.mult)
                elif j == 11:
                    v.tensor_scalar(posi[:, 0], pos[:], 4, None, ALU.logical_shift_right)
                    v.tensor_scalar(posi[:, 1], pos[:], 15, None, ALU.bitwise_and)
                    ins = v.tensor_copy(lidf[:], lidx[:])
                elif j == 12:
                    ins = v.tensor_copy(posf[:], posi[:])
                elif j == 13:
                    ins = v.tensor_tensor(hot[:], iota16[:].unsqueeze(1).unsqueeze(1).broadcast_to([P, 2, TOPK, TOPK]),
                                          posf[:].unsqueeze(3).broadcast_to([P, 2, TOPK, TOPK]), ALU.is_equal)
                elif j == 14:
                    ins = v.tensor_tensor(hot[:], hot[:], lidf[:].unsqueeze(2).broadcast_to([P, 2, TOPK, TOPK]), ALU.mult)
                else:
                    ins = v.tensor_reduce(picked[:].rearrange("p q k -> p (q k)"),
                                          hot[:].rearrange("p q k i -> p (q k) i"), AX.X, ALU.add)
                ins.then_inc(topk_step, 1)

            def numbers(m):
                dve.wait_ge(topk_step, TK * (m + 1))
                if m >= 2:
                    dve.wait_ge(v_used_pe, VS // 2 + (m - 1) * ODD)
                    dve.wait_ge(v_used_dve, VS // 2 + (m - 1) * ODD)
                v.scalar_tensor_tensor(out=idx[:, m % 2, :], in0=picked[:, 0, :], scalar=float(NK),
                                       in1=picked[:, 1, :], op0=ALU.mult, op1=ALU.add).then_inc(idx_ready, 1)

            def dot(n, k):
                i = n // NH
                if n % NH == 0 and k == 0:
                    dve.wait_ge(h_in, 16 * (i + 1))
                dve.wait_ge(u_in[k % US], (n * (TOPK // US) + k // US + 1) * 16)
                row = ubuf[:, k % US, :]
                v.scalar_tensor_tensor(out=row, in0=row, scalar=1.0, in1=hbuf[:, i % 2, :], op0=ALU.mult, op1=ALU.mult,
                                       accum_out=dots[:, n % 2, k:k + 1]).then_inc(u_used, 1)

            def weights(n):
                dve.wait_ge(topk_exp, n + 1)
                v.reciprocal(ginv[:, n % 2, :], gsum[:, n % 2, :]).then_inc(wts_step, 1)
                dve.wait_ge(gelu_done, n + 1)
                dve.wait_ge(wts_step, 2 * n + 1)
                v.scalar_tensor_tensor(out=wts[:, n % 2, :], in0=gel[:, n % 2, :], scalar=ginv[:, n % 2, :],
                                       in1=gexp[:, n % 2, :], op0=ALU.mult, op1=ALU.mult).then_inc(wts_step, 1)

            def add_row(n, kk):
                k = 2 * kk
                if n % NH == 0 and kk == 0:
                    dve.wait_ge(acc_in, 16 * (n // NH + 1))
                if kk == 0:
                    dve.wait_ge(wts_step, 2 * (n + 1))
                dve.wait_ge(v_used_dve, VS // 2 + n * ODD + kk)
                dve.wait_ge(v_in[k % VS], (n * (TOPK // VS) + k // VS + 1) * 16)
                v.scalar_tensor_tensor(out=acc[:], in0=vbuf[:, k % VS, :], scalar=wts[:, n % 2, k:k + 1], in1=acc[:],
                                       op0=ALU.mult, op1=ALU.add).then_inc(v_used_dve, 1)

            v.memset(eps[:], EPS).then_inc(setup, 1)
            v.memset(aT[:], 1.0).then_inc(setup, 1)
            v.memset(skT[:, :, 0:CHUNK], 0.0).then_inc(setup, 1)
            v.memset(sv[:, 0, :], 0.0).then_inc(setup, 1)
            v.memset(probs[:], 0.0).then_inc(setup, 1)
            v.memset(state[:, 1], 0.0).then_inc(setup, 1)
            dve.sem_inc(u_used, US)
            dve.sem_inc(v_used_dve, VS // 2)
            dve.sem_inc(v_used_pe, VS // 2)
            dve.wait_ge(setup, SETUP)
            dve.wait_ge(const_in, CONST_READY)
            for n in range(FIRST, LAST + 1):
                peer = 0 <= n < NHEAD
                for k in range(TOPK):
                    if peer:
                        dot(n, k)
                    if 0 <= n + 1 < NHEAD:
                        topk(n + 1, k)
                if 0 <= n + 1 < NHEAD:
                    numbers(n + 1)
                if peer:
                    weights(n)
                    for kk in range(ODD // 2):
                        add_row(n, kk)
                if n > FIRST:
                    stage_parts(n - 1)
                if peer:
                    for kk in range(ODD // 2, ODD):
                        add_row(n, kk)
                    if n % NH == NH - 1:
                        dve.wait_ge(v_used_dve, VS // 2 + (n + 1) * ODD)
                        dve.wait_ge(v_used_pe, VS // 2 + (n + 1) * ODD)
                        if n // NH:
                            dve.wait_ge(tail_out, 16 * (n // NH))
                        v.tensor_tensor(tX[:].rearrange("p (c n) -> p c n", c=2), acc[:].rearrange("p (c n) -> p c n", c=2),
                                        ysum[:], ALU.add).then_inc(x2_done, 1)


WEXP = 2 * GROUP + 1


def shape_tables():
    q = np.arange(P)[:, None]
    k = np.arange(P)[None, :]
    tri = ((q // CHUNK == k // CHUNK) & (q > k)).astype(np.float32)
    chunk_of = (q // CHUNK == np.arange(2)[None, :]).astype(np.float32)
    col = np.arange(BAND)[None, :]
    near = (col // CHUNK == q // CHUNK) | (col // CHUNK == q // CHUNK + 1)
    far = np.abs(q - (col - CHUNK)).astype(np.float32)
    later = np.where(near, far, FAR).astype(np.float32)
    first = np.where(near & (col >= CHUNK), far, FAR).astype(np.float32)
    return {"ident": np.eye(P, dtype=np.float32), "tri": tri, "chunk_of": chunk_of,
            "dist": np.stack([first, later], 1), "iota16": np.arange(TOPK, dtype=np.float32)}


def kernel(**inputs):
    import concourse.bacc as bacc
    from concourse.bass_utils import run_bass_kernel_spmd

    a = {k: np.asarray(v) for k, v in inputs.items()}

    def feature_major(g, n):
        return np.ascontiguousarray(g.reshape(n, P).T)

    def by_rows(w):
        return w.reshape(-1, P, w.shape[1]).transpose(1, 0, 2).reshape(P, -1)

    w = a["w_in"][0]
    at = np.cumsum([0, 512, 512, 1024, 1024, GRANK, 1024, 256, 256])
    gq, gk, gvw, grw, ga, sq, sk, svw = (w[:, at[i]:at[i + 1]] for i in range(8))
    order = [4 * (2 * (f // GROUP) + half) + f % GROUP for f in range(8) for half in range(2)]
    sq = sq.reshape(D, QH, HD)[:, order].reshape(D, D)
    swo = a["w_swa_out"][0].reshape(QH, HD, D)[order].reshape(D, D)
    bg, glo, wo, wq, pg = a["w_branch_gate"][0], a["w_gla_out"][0], a["w_out"][0], a["peer_wq"][0], a["w_ple_gate"][0]
    H = 512
    parts = {"gk": gk, "gv0": gvw[:, :H], "gv1": gvw[:, H:], "gq": gq, "gr0": grw[:, :H], "gr1": grw[:, H:],
             "kv": np.concatenate([sk, svw], 1), "sq0": sq[:, :H], "sq1": sq[:, H:]}
    for q in range(2):
        c = slice(q * H, q * H + H)
        parts.update({f"bgg{q}": bg[:, c], f"bgs{q}": bg[:, D + q * H:D + q * H + H], f"glo{q}": glo[:, c],
                      f"swo{q}": swo[:, c], f"wo{q}": wo[:, c], f"pg{q}": pg[:, c]})
    for q in range(4):
        parts[f"wq{q}"] = wq[:, q * H:q * H + H]
    slabs = np.zeros((len(SLABS), P, KT * SW), np.float32)
    for n, name in enumerate(SLABS):
        if name == "pp":
            slabs[n, :, :2048] = by_rows(a["w_ple_proj"][0])
        else:
            slabs[n] = by_rows(parts[name])

    arrays = {
        "x": a["x"].reshape(SEQ, D), "slabs": slabs,
        "pT": a["p"].reshape(SEQ, 2, P).transpose(2, 1, 0),
        "g_mix": feature_major(a["norm_mix"][0], KT), "g_ple": feature_major(a["norm_ple"][0], KT),
        "g_on": feature_major(a["gla_onorm"][0], 2), "b_bg": feature_major(a["b_branch_gate"][0], 2 * KT),
        "sinks": a["swa_sinks"][0], "g_ffn": a["norm_ffn"][0], "g_fin": a["norm_final"],
        "wga": by_rows(ga).reshape(P, KT, GRANK),
        "wa2": np.concatenate([a["w_gla_a2"][0], a["b_gla_a"]], 0),
        "subk": a["peer_subkeys"][0].transpose(2, 0, 1),
        "u": a["peer_u"][0], "v": a["peer_v"][0], **shape_tables(),
    }
    arrays = {k: np.ascontiguousarray(v) for k, v in arrays.items()}
    nc = bacc.Bacc("TRN2", target_bir_lowering=False, num_devices=1)
    aps = {k: nc.dram_tensor(f"in_{k}", v.shape, F32, kind="ExternalInput").ap() for k, v in arrays.items()}
    out = nc.dram_tensor("out_0", (SEQ, D), F32, kind="ExternalOutput").ap()
    build(nc, aps, out)
    r = run_bass_kernel_spmd(nc, [{f"in_{k}": v for k, v in arrays.items()}], core_ids=[0])
    return r.results[0]["out_0"].reshape(1, SEQ, D)
```

```python
from contextlib import ExitStack

import numpy as np

import concourse.bass as bass
from concourse import mybir

ALU = mybir.AluOpType
ACT = mybir.ActivationFunctionType
AX = mybir.AxisListType
F32 = mybir.dt.float32
U32 = mybir.dt.uint32

P = 128
D = 1024
KT = D // P
SEQ = 1024
SEG = 256
NSEG = SEQ // SEG
TT = SEG // P
NTILE = SEQ // P
CHUNK = 64
EPS = 1e-6

GH, GDK, GDV, GRANK, GTEMP = 4, 128, 256, 16, 16.0
QH, KVH, HD = 16, 4, 64
GROUP = QH // KVH
BAND = 3 * CHUNK
FAR = 1e33

NH, NK, TOPK = 8, 128, 16
NHEAD = NTILE * NH
LOW = -3.0e38
SW = 512
RS = 2
US, VS, DS = 4, 8, 3
ODD = TOPK // 2
TK = 11

FRONT = [
    (0, []),
    (7, []),
    (7, [("gk", 2), ("gv0", 4)]),
    (4, [("gv1", 2), ("gq", 4)]),
    (4, [("gr0", 2), ("gr1", 4)]),
    (6, [("kv", 2), ("sq0", 6)]),
    (0, []),
    (6, [("sq1", 2), ("bgg0", 6)]),
    (4, [("glo0", 2), ("bgg1", 4)]),
    (8, [("glo1", 2)]),
    (8, [("bgs0", 2)]),
    (8, [("bgs1", 2)]),
    (10, [("swo0", 8), ("swo1", 10)]),
    (4, [("wo0", 2), ("wo1", 4)]),
    (0, []),
    (8, [("wq0", 6)]),
    (8, [("wq1", 2), ("wq2", 6)]),
    (4, [("wq3", 2)]),
]
TAIL = [(0, []), (12, [("pg0", 6), ("pg1", 8), ("pp", 12)]), (0, [])]
SCORED = [15, 16, 16, 17]
SLABS = [w for _, ws in FRONT + TAIL for w, _ in ws]

LEAD = 18
FIRST, LAST = -LEAD, NHEAD + 6


def stages(n):
    s, j = divmod(n + LEAD, 16)
    found = []
    if j < len(FRONT) - 16 and 1 <= s <= NSEG:
        found.append(("front", s - 1, 16 + j))
    if 0 <= s < NSEG:
        found.append(("front", s, j))
    s, j = divmod(n - 19, 16)
    if 0 <= s < NSEG and j < 3:
        found.append(("tail", s, j))
    return found


def table(kind):
    return FRONT if kind == "front" else TAIL


def uses_through(n):
    return sum(table(k)[j][0] for m in range(FIRST, n + 1) for k, _, j in stages(m))


def uses_at(kind, which, stage):
    total = 0
    for m in range(FIRST, LAST + 1):
        for item in stages(m):
            total += table(item[0])[item[2]][0]
            if item == (kind, which, stage):
                return total


def slab_reads():
    total, found = 0, []
    for n in range(FIRST, LAST + 1):
        for k, _, j in stages(n):
            found += [(w, n, total + u) for w, u in table(k)[j][1]]
            total += table(k)[j][0]
    return found


SLAB_READS = slab_reads()


class Count:

    def __init__(self):
        self.n = 0

    def next(self):
        self.n += 1
        return self.n


def build(nc, a, out):
    with ExitStack() as ctx:
        def sb(name, shape, dt=F32):
            return ctx.enter_context(nc.sbuf_tensor(name, shape, dt))

        def ps(name, shape):
            return ctx.enter_context(nc.psum_tensor(name, shape, F32))

        def sem(name):
            return ctx.enter_context(nc.semaphore(name))

        def dram(name, shape):
            return nc.dram_tensor(name, shape, F32, kind="Internal").ap()

        x1_d = dram("x1_d", (NTILE, P, D))

        ident = sb("ident", [P, P])
        tri = sb("tri", [P, P])
        chunk_of = sb("chunk_of", [P, 2])
        dist = sb("dist", [P, 2, BAND])
        iota16 = sb("iota16", [P, TOPK])
        g_mix = sb("g_mix", [P, KT])
        g_ple = sb("g_ple", [P, KT])
        g_on = sb("g_on", [P, 2])
        b_bg = sb("b_bg", [P, 2 * KT])
        sinks = sb("sinks", [P, QH])
        g_ffn = sb("g_ffn", [P, D])
        wga = sb("wga", [P, KT, GRANK])
        wa2 = sb("wa2", [GRANK + 1, GH * GDK])
        subk = sb("subk", [P, 2, NK])
        eps = sb("eps", [P, 1])

        slab = sb("slab", [P, RS, KT * SW])
        hT = sb("hT", [P, KT, SEG])
        rX = sb("rX", [P, 2048])
        rA = sb("rA", [P, 2048])
        rB = sb("rB", [P, 2048])
        rC = sb("rC", [P, 2048])
        rD = sb("rD", [P, 2048])
        rE = sb("rE", [P, 2048])
        xs = rX[:].rearrange("p (t n) -> p t n", t=TT)
        sl = rX[:, 0:2 * GROUP * BAND].rearrange("p (j n) -> p j n", n=BAND)
        gv = rA[:].rearrange("p (t n) -> p t n", t=TT)
        sqT = rA[:].rearrange("p (f n) -> p f n", f=8)
        ysw = rA[:]
        gr = rB[:].rearrange("p (t n) -> p t n", t=TT)
        yswT = rB[:].rearrange("p (f n) -> p f n", f=8)
        ysc = rB[:].rearrange("p (b t n) -> p b t n", b=2, t=TT)
        yglT = rC[:].rearrange("p (f n) -> p f n", f=8)
        h2 = rC[:].rearrange("p (t n) -> p t n", t=TT)
        gqT = rD[:, 0:1024].rearrange("p (h n) -> p h n", h=GH)
        kdec = rD[:, 1024:2048].rearrange("p (t n) -> p t n", t=TT)
        mT = rD[:].rearrange("p (f n) -> p f n", f=8)
        pq = rD[:].rearrange("p (b f n) -> p b f n", b=2, f=4)
        loga = rE[:, 0:1024].rearrange("p (t n) -> p t n", t=TT)
        zs = rE[:, 1024:2048].rearrange("p (t n) -> p t n", t=TT)
        gates = rE[:].rearrange("p (f n) -> p f n", f=8)
        tgate = rX[:].rearrange("p (t n) -> p t n", t=TT)
        thT = rE[:].rearrange("p (f n) -> p f n", f=8)
        g_fin = rE[:, 1024:2048]
        skT = sb("skT", [P, 2, CHUNK + SEG])
        sv = sb("sv", [P, TT + 1, KVH * HD])
        aT = sb("aT", [GRANK + 1, SEG])
        dec = sb("dec", [P, GH, 2 * TT])
        state = sb("state", [P, 2, GH, GDV])
        stat_x = sb("stat_x", [P, 3, TT])
        stat_h = sb("stat_h", [P, 3, TT])
        stat_t = sb("stat_t", [P, 3, 2 * TT])
        gstat = sb("gstat", [P, 3, GH])
        otok = sb("otok", [P, GH * GDV])
        ygl = otok[:]
        probs = sb("probs", [P, 2 * GROUP, 256])
        junk = probs[:, :, CHUNK:CHUNK + P]
        pT = sb("pT", [P, GROUP, 2, P])
        ths = [pT[:].rearrange("p j b n -> p (j b) n"), probs[:, :, CHUNK:CHUNK + P]]
        sm = sb("sm", [P, 5, 2 * GROUP])
        tX = sb("tX", [P, TT, D])
        tpT = sb("tpT", [P, 2, SEG])

        ubuf = sb("ubuf", [P, US, D])
        vbuf = sb("vbuf", [P, VS, D])
        hbuf = sb("hbuf", [P, 2, D])
        acc = sb("acc", [P, D])
        diag = sb("diag", [P, DS, P])
        vals = sb("vals", [P, TT, NH, 2, TOPK])
        lidx = sb("lidx", [P, TT, NH, 2, TOPK], U32)
        lidf = sb("lidf", [P, 2, TOPK])
        tv = sb("tv", [P, TOPK])
        negmax = sb("negmax", [P, 1])
        pos = sb("pos", [P, TOPK], U32)
        posi = sb("posi", [P, 2, TOPK], U32)
        posf = sb("posf", [P, 2, TOPK])
        hot = sb("hot", [P, 2, TOPK, TOPK])
        cand = hot[:, 0].rearrange("p i j -> p (i j)")
        picked = sb("picked", [P, 2, TOPK])
        idx = sb("idx", [P, 2, TOPK], U32)
        gexp = sb("gexp", [P, 2, TOPK])
        gsum = sb("gsum", [P, 2, 1])
        ginv = sb("ginv", [P, 2, 1])
        dots = sb("dots", [P, 2, TOPK])

        bank = ps("bank", [P, 2, 512])
        wide = ps("wide", [P, 4, 512])
        ysum = ps("ysum", [P, 2, 512])

        const_in = sem("const_in")
        setup = sem("setup")
        x_in = sem("x_in")
        xres_in = sem("xres_in")
        slab_in = [sem(f"slab_in{i}") for i in range(RS)]
        bank_full = sem("bank_full")
        emptied = sem("emptied")
        vec_step = sem("vec_step")
        vec_done = sem("vec_done")
        squared = sem("squared")
        root_done = sem("root_done")
        scaled = sem("scaled")
        tail_scaled = sem("tail_scaled")
        gate_step = sem("gate_step")
        u_full = sem("u_full")
        o_full = sem("o_full")
        logit_full = sem("logit_full")
        window_exp = sem("window_exp")
        x1_out = sem("x1_out")
        h_in = sem("h_in")
        h_ready = sem("h_ready")
        acc_in = sem("acc_in")
        topk_step = sem("topk_step")
        topk_exp = sem("topk_exp")
        idx_ready = sem("idx_ready")
        held = sem("held")
        u_in = [sem(f"u_in{i}") for i in range(US)]
        v_in = [sem(f"v_in{i}") for i in range(VS)]
        u_used = sem("u_used")
        v_used_dve = sem("v_used_dve")
        v_used_pe = sem("v_used_pe")
        gelu_done = sem("gelu_done")
        wts_step = sem("wts_step")
        diag_done = sem("diag_done")
        x2_done = sem("x2_done")
        tp_in = sem("tp_in")
        gfin_in = sem("gfin_in")
        tail_out = sem("tail_out")

        consts = [(ident[:], a["ident"]), (tri[:], a["tri"]), (chunk_of[:], a["chunk_of"]),
                  (dist[:], a["dist"]), (iota16[:], a["iota16"].partition_broadcast(P)),
                  (g_mix[:], a["g_mix"]), (g_ple[:], a["g_ple"]), (g_on[:], a["g_on"]),
                  (b_bg[:], a["b_bg"]), (sinks[:], a["sinks"].partition_broadcast(P)),
                  (g_ffn[:], a["g_ffn"].partition_broadcast(P)), (wga[:], a["wga"]),
                  (wa2[:], a["wa2"]), (subk[:], a["subk"])]
        CONST_READY = 16 * len(consts)
        SETUP = 6

        x_t = a["x"].rearrange("(t p) d -> p t d", p=P)
        out_t = out.rearrange("(t p) d -> t p d", p=P)
        uw = [wide[:, 2 * b:2 * b + 2, :].rearrange("p b (h n) -> p (b h) n", h=2) for b in range(2)]
        ow = uw[0]

        def done_before(n):
            return n - FIRST

        block = ctx.enter_context(nc.Block())

        @block.sync
        def _(sp):
            def tiles(t, s):
                return t[TT * s:TT * s + TT].rearrange("t p d -> p t d")

            def front(s, j):
                if j == 12:
                    sp.wait_ge(window_exp, WEXP * (4 * s + 4))
                    sp.dma_start(xs, x_t[:, TT * s:TT * s + TT, :]).then_inc(xres_in, 16)
                if j == 15:
                    sp.wait_ge(vec_done, done_before(16 * s - LEAD + 15))
                    sp.dma_start(tiles(x1_d, s), xs).then_inc(x1_out, 16)
                    if s + 1 < NSEG:
                        sp.wait_ge(x1_out, 16 * (s + 1))
                        sp.dma_start(xs, x_t[:, TT * s + TT:TT * s + 2 * TT, :]).then_inc(x_in, 16)

            loaded = Count()

            def slabs_for(n):
                for m, (name, slot, _) in enumerate(SLAB_READS):
                    if slot == n:
                        if m >= RS:
                            sp.wait_ge(bank_full, SLAB_READS[m - RS][2])
                        w = 2 * D if name == "pp" else KT * SW
                        sp.dma_start(slab[:, m % RS, 0:w], a["slabs"][SLABS.index(name), :, 0:w]
                                     ).then_inc(slab_in[m % RS], 16)
                        loaded.next()

            sp.dma_start(xs, x_t[:, 0:TT, :]).then_inc(x_in, 16)
            for dst, src in consts:
                sp.dma_start(dst, src).then_inc(const_in, 16)
            for n in range(FIRST, LAST + 1):
                before = stages(n - 1)
                i, h = divmod(n + 2, NH)
                if h == 0 and 0 <= i < NTILE:
                    sp.wait_ge(x1_out, 16 * (i // TT + 1))
                    if i >= 2:
                        sp.wait_ge(u_used, US + (i - 1) * NH * TOPK)
                    sp.dma_start(hbuf[:, i % 2, :], x1_d[i]).then_inc(h_in, 16)
                i, h = divmod(n, NH)
                if h == 0 and 0 <= i < NTILE:
                    if i:
                        sp.wait_ge(x2_done, i)
                    sp.wait_ge(x1_out, 16 * (i // TT + 1))
                    sp.dma_start(acc[:], x1_d[i]).then_inc(acc_in, 16)
                for kind, s, j in stages(n + 1):
                    if kind == "tail" and j == 0:
                        if s:
                            sp.wait_ge(bank_full, uses_at("tail", s - 1, 1))
                        sp.dma_start(tpT[:], a["pT"][:, :, s * SEG:s * SEG + SEG]).then_inc(tp_in, 16)
                for kind, i, j in before:
                    if kind == "tail" and j == 1:
                        sp.wait_ge(bank_full, uses_at("tail", i, 1))
                        sp.dma_start(g_fin, a["g_fin"].partition_broadcast(P)).then_inc(gfin_in, 16)
                for kind, i, j in stages(n - 2):
                    if kind == "tail" and j == 2:
                        sp.wait_ge(vec_done, done_before(n - 1))
                        sp.dma_start(tiles(out_t, i), tX[:]).then_inc(tail_out, 16)
                for kind, s, j in stages(n):
                    if kind == "front":
                        front(s, j)
                slabs_for(n + 1)
            assert loaded.n == len(SLAB_READS)
            sp.wait_ge(vec_done, done_before(LAST))
            sp.dma_start(tiles(out_t, NSEG - 1), tX[:]).then_inc(tail_out, 16)
            sp.wait_ge(tail_out, 16 * NSEG)

        @block.gpsimd
        def _(pool):
            def hold(s, value):
                pool.wait_ge(s, value)
                pool.sem_inc(held, 1)

            def gather(rows, dst, b, k, done):
                nc.gpsimd.indirect_dma_start(
                    out=dst, out_offset=None, in_=rows,
                    in_offset=bass.IndirectOffsetOnAxis(ap=idx[:, b, k:k + 1], axis=0)).then_inc(done, 16)

            with nc.gpsimd.Fori(0, NHEAD // 2) as i:
                for b in range(2):
                    hold(idx_ready, i * 2 + b + 1)
                    for k in range(TOPK):
                        hold(u_used, i * (2 * TOPK) + b * TOPK + k + 1)
                        gather(a["u"], ubuf[:, k % US, :], b, k, u_in[k % US])
                    for k in range(TOPK):
                        hold(v_used_pe if k % 2 else v_used_dve, i * TOPK + b * ODD + k // 2 + 1)
                        gather(a["v"], vbuf[:, k % VS, :], b, k, v_in[k % VS])

        @block.tensor
        def _(pe):
            mm = nc.tensor.matmul
            used = Count()
            slabs = Count()

            def bank_for():
                n = used.next() - 1
                if n >= 2:
                    pe.wait_ge(emptied, n - 1)
                return bank[:, n % 2, :]

            def all_emptied():
                pe.wait_ge(emptied, used.n)

            def after_vector(n):
                pe.wait_ge(vec_done, done_before(n))

            def next_slab():
                n = slabs.next() - 1
                pe.wait_ge(slab_in[n % RS], 16 * (n // RS + 1))
                return slab[:, n % RS, :].rearrange("p (k n) -> p k n", k=KT)

            def turned(src):
                for f in range(0, KT, 2):
                    b = bank_for()
                    for g in range(2):
                        for t in range(TT):
                            c0 = g * SEG + t * P
                            m = nc.tensor.transpose(b[:, c0:c0 + P], src[:, t, (f + g) * P:(f + g) * P + P], ident[:])
                    m.then_inc(bank_full, 1)

            def by_feature(w, tiles, src):
                for f in range(0, tiles, 2):
                    b = bank_for()
                    for g in range(2):
                        for k in range(KT):
                            m = mm(b[:, g * SEG:g * SEG + SEG], w[:, k, (f + g) * P:(f + g) * P + P], src[:, k, :],
                                   start=(k == 0), stop=(k == KT - 1))
                    m.then_inc(bank_full, 1)

            def by_token(w, src):
                for t in range(TT):
                    b = bank_for()
                    for k in range(KT):
                        m = mm(b, src[:, k, t * P:t * P + P], w[:, k, :], start=(k == 0), stop=(k == KT - 1))
                    m.then_inc(bank_full, 1)

            def u_of(t):
                for half in range(2):
                    r0 = half * CHUNK
                    for h in range(GH):
                        m = mm(uw[half][:, h, :], kdec[r0:r0 + CHUNK, t, h * GDK:h * GDK + GDK],
                               gv[r0:r0 + CHUNK, t, h * GDV:h * GDV + GDV], start=True, stop=True)
                    m.then_inc(u_full, 1)

            def o_of(t):
                for half in range(2):
                    r0 = half * CHUNK
                    c0 = t * P + r0
                    for h in range(GH):
                        m = mm(ow[r0:r0 + CHUNK, h, :], gqT[:, h, c0:c0 + CHUNK], state[:, half, h, :],
                               start=True, stop=True)
                m.then_inc(o_full, 1)

            def turn_o():
                for odd in range(2):
                    b = bank_for()
                    for j in range(4):
                        f = 2 * j + odd
                        m = nc.tensor.transpose(b[:, j * P:j * P + P], otok[:, f * P:f * P + P], ident[:])
                    m.then_inc(bank_full, 1)

            def logits(batch):
                t = batch // 2
                for e in range(2):
                    g = 2 * (batch % 2) + e
                    r0 = (g % 2) * HD
                    for j in range(GROUP):
                        o = wide[:, 2 * e + j // 2, (j % 2) * BAND:(j % 2) * BAND + BAND]
                        m = mm(o, sqT[r0:r0 + HD, (g // 2) * GROUP + j, t * P:t * P + P],
                               skT[r0:r0 + HD, g // 2, t * P:t * P + BAND], start=True, stop=True)
                m.then_inc(logit_full, 1)

            def values(batch):
                t = batch // 2
                for e in range(2):
                    g = 2 * (batch % 2) + e
                    r0 = (g % 2) * HD
                    for half in range(2):
                        b = bank_for()
                        for j in range(2):
                            for blk in range(2):
                                c0 = (2 * j + blk) * P
                                m = nc.tensor.transpose(b[:, c0:c0 + P], probs[:, GROUP * e + 2 * half + j,
                                                                              blk * P:blk * P + P], ident[:])
                        m.then_inc(bank_full, 1)
                    all_emptied()
                    b = bank_for()
                    for blk in range(2):
                        m = mm(b[r0:r0 + HD, :], sv[:, t + blk, g * HD:g * HD + HD], pT[:, :, blk, :],
                               start=(blk == 0), stop=(blk == 1))
                    m.then_inc(bank_full, 1)

            def front(n, s, j):
                if j == 1:
                    pe.wait_ge(scaled, TT * (s + 1))
                    turned(xs)
                    all_emptied()
                    b = bank_for()
                    for k in range(KT):
                        m = mm(b[0:GRANK, 0:SEG], wga[:, k, :], hT[:, k, :], start=(k == 0), stop=(k == KT - 1))
                    m.then_inc(bank_full, 1)
                    all_emptied()
                    for t in range(TT):
                        mm(bank_for(), aT[:, t * P:t * P + P], wa2[:], start=True, stop=True).then_inc(bank_full, 1)
                elif j == 2:
                    by_token(next_slab(), hT)
                    by_token(next_slab(), hT)
                    after_vector(n)
                    b = bank_for()
                    for t in range(TT):
                        for h in range(GH):
                            c0 = h * 2 * TT + 2 * t
                            m = mm(b[:, c0:c0 + 2], loga[:, t, h * GDK:h * GDK + GDK], chunk_of[:],
                                   start=True, stop=True)
                    m.then_inc(bank_full, 1)
                    for t in range(TT):
                        mm(bank_for(), tri[:], loga[:, t, :], start=True, stop=True).then_inc(bank_full, 1)
                elif j == 3:
                    by_token(next_slab(), hT)
                    by_feature(next_slab(), 4, hT)
                    all_emptied()
                    after_vector(n)
                    u_of(0)
                elif j == 4:
                    by_token(next_slab(), hT)
                    by_token(next_slab(), hT)
                    after_vector(n)
                    o_of(0)
                elif j == 5:
                    w = next_slab()
                    by_feature(w, 2, hT)
                    b = bank_for()
                    for t in range(TT):
                        for k in range(KT):
                            m = mm(b[:, t * 256:t * 256 + 256], hT[:, k, t * P:t * P + P], w[:, k, 256:512],
                                   start=(k == 0), stop=(k == KT - 1))
                    m.then_inc(bank_full, 1)
                    after_vector(n)
                    turn_o()
                    u_of(1)
                    by_feature(next_slab(), 4, hT)
                elif j == 6:
                    after_vector(n)
                    o_of(1)
                elif j == 7:
                    by_feature(next_slab(), 4, hT)
                    after_vector(n)
                    turn_o()
                    by_feature(next_slab(), 4, hT)
                    pe.wait_ge(emptied, used.n - 2)
                    logits(0)
                elif j == 8:
                    by_feature(next_slab(), 4, yglT)
                    by_feature(next_slab(), 4, hT)
                    after_vector(n)
                    logits(1)
                elif j in (9, 10, 11):
                    by_feature(next_slab(), 4, yglT if j == 9 else hT)
                    after_vector(n)
                    if j < 11:
                        logits(j - 7)
                    values(j - 9)
                elif j == 12:
                    after_vector(n)
                    values(3)
                    all_emptied()
                    by_feature(next_slab(), 4, yswT)
                    by_feature(next_slab(), 4, yswT)
                elif j == 13:
                    after_vector(n)
                    by_token(next_slab(), mT)
                    by_token(next_slab(), mT)
                elif j >= 15:
                    if j == 15:
                        after_vector(n)
                        turned(h2)
                        all_emptied()
                    for b2 in [q % 2 for q in range(4) if SCORED[q] == j]:
                        by_feature(next_slab(), 4, hT)
                        all_emptied()
                        for t in range(TT):
                            b = bank_for()
                            for f in range(4):
                                m = mm(b[:, f * P:f * P + P], pq[:, b2, f, t * P:t * P + P], subk[:, f % 2, :],
                                       start=True, stop=True)
                            m.then_inc(bank_full, 1)

            def tail(n, i, j):
                if j != 1:
                    return
                pe.wait_ge(tail_scaled, TT * (i + 1))
                for f in range(0, KT, 2):
                    b = bank_for()
                    for g in range(2):
                        for t in range(TT):
                            c0 = g * SEG + t * P
                            m = nc.tensor.transpose(b[:, c0:c0 + P], ths[t][:, f + g, :], ident[:])
                    m.then_inc(bank_full, 1)
                all_emptied()
                by_token(next_slab(), thT)
                by_token(next_slab(), thT)
                w = next_slab().rearrange("p k n -> p (k n)")[:, 0:2 * D].rearrange("p (k n) -> p k n", k=2)
                pe.wait_ge(tp_in, 16 * (i + 1))
                for q in range(2):
                    for t in range(TT):
                        b = bank_for()
                        for k in range(2):
                            m = mm(b, tpT[:, k, t * P:t * P + P], w[:, k, q * 512:q * 512 + 512],
                                   start=(k == 0), stop=(k == 1))
                        m.then_inc(bank_full, 1)

            def peer_head(n):
                i, h = divmod(n, NH)
                if h == 0 and i:
                    pe.wait_ge(x2_done, i)
                for kk in range(ODD):
                    k = 2 * kk + 1
                    m0 = n * ODD + kk
                    pe.wait_ge(diag_done, m0 + 1)
                    pe.wait_ge(v_in[k % VS], (n * (TOPK // VS) + k // VS + 1) * 16)
                    for c in range(2):
                        m = mm(ysum[:, c, :], diag[:, m0 % DS, :], vbuf[:, k % VS, c * 512:c * 512 + 512],
                               start=(h == 0 and kk == 0), stop=(h == NH - 1 and kk == ODD - 1))
                    m.then_inc(v_used_pe, 1)

            pe.wait_ge(const_in, CONST_READY)
            pe.wait_ge(setup, SETUP)
            for n in range(FIRST, LAST + 1):
                if 0 <= n < NHEAD:
                    peer_head(n)
                for kind, s, j in stages(n):
                    (front if kind == "front" else tail)(n, s, j)
                assert used.n == uses_through(n)

        @block.scalar
        def _(act):
            fn = nc.scalar.activation
            used = Count()
            squares = Count()
            roots = Count()
            gate_ops = Count()
            exps = Count()

            def full():
                n = used.next()
                act.wait_ge(bank_full, n)
                return bank[:, (n - 1) % 2, :]

            def after_vector(n):
                act.wait_ge(vec_done, done_before(n))

            def copied(dst, src, **kw):
                fn(dst, src, kw.pop("func", ACT.Copy), **kw).then_inc(emptied, 1)

            def square_sums(pieces):
                for src, dst in pieces:
                    if squares.n:
                        act.wait_ge(squared, squares.n)
                    squares.next()
                    fn(junk[:, 0:src.shape[-1] // P, :], src.rearrange("p (j n) -> p j n", n=P), ACT.Square,
                       accum_out=dst).then_inc(squared, 1)
                act.wait_ge(squared, squares.n)

            def root(dst, src, width):
                roots.next()
                fn(dst, src, ACT.Sqrt, bias=eps[:], scale=1.0 / width).then_inc(root_done, 1)

            def window_exps():
                for j in range(2 * GROUP):
                    exps.next()
                    fn(probs[:, j, CHUNK:256], sl[:, j, :], ACT.Exp, bias=sm[:, 1, j:j + 1],
                       accum_out=sm[:, 3, j:j + 1]).then_inc(window_exp, 1)
                exps.next()
                fn(sm[:, 4, :], sm[:, 2, :], ACT.Exp).then_inc(window_exp, 1)

            def sigmoids(f0, b0):
                for f in range(0, 4, 2):
                    b = full()
                    for g in range(2):
                        m = fn(gates[:, f0 + f + g, :], b[:, g * SEG:g * SEG + SEG], ACT.Sigmoid,
                               bias=b_bg[:, b0 + f + g:b0 + f + g + 1])
                    m.then_inc(emptied, 1)

            def window_out(batch):
                t = batch // 2
                for e in range(2):
                    g = 2 * (batch % 2) + e
                    r0 = (g % 2) * HD
                    for half in range(2):
                        copied(pT[:, 2 * half:2 * half + 2, :, :].rearrange("p j b n -> p (j b n)"), full())
                    copied(yswT[r0:r0 + HD, (g // 2) * GROUP:(g // 2) * GROUP + GROUP, t * P:t * P + P],
                           full()[r0:r0 + HD, :].rearrange("p (j n) -> p j n", j=GROUP))

            def turn_o(t):
                for odd in range(2):
                    copied(yglT[:, odd:8:2, t * P:t * P + P], full().rearrange("p (f n) -> p f n", f=4),
                           scale=g_on[:, odd:odd + 1])

            def o_stats():
                square_sums([(ow[:, h, :], gstat[:, 0, h:h + 1]) for h in range(GH)])
                root(gstat[:, 1, :], gstat[:, 0, :], GDV)

            def front(n, s, j):
                if j == 0:
                    act.wait_ge(x_in, 16 * (s + 1))
                    if n > FIRST:
                        after_vector(n)
                    square_sums([(xs[:, t, :], stat_x[:, 0, t:t + 1]) for t in range(TT)])
                    root(stat_x[:, 1, :], stat_x[:, 0, :], D)
                elif j == 1:
                    after_vector(n)
                    for t in range(TT):
                        fn(xs[:, t, :], xs[:, t, :], ACT.Copy, scale=stat_x[:, 2, t:t + 1]).then_inc(scaled, 1)
                    for f in range(0, KT, 2):
                        b = full()
                        for g in range(2):
                            m = fn(hT[:, f + g, :], b[:, g * SEG:g * SEG + SEG], ACT.Copy, scale=g_mix[:, f + g:f + g + 1])
                        m.then_inc(emptied, 1)
                    copied(aT[0:GRANK, :], full()[0:GRANK, 0:SEG])
                    for t in range(TT):
                        b = full()
                        fn(zs[:, t, :], b, ACT.Copy)
                        copied(loga[:, t, :], b, func=ACT.Abs)
                    act.wait_ge(emptied, used.n)
                    gate_ops.next()
                    fn(loga, loga, ACT.Exp, scale=-1.0).then_inc(gate_step, 1)
                    act.wait_ge(gate_step, gate_ops.n)
                    gate_ops.next()
                    fn(loga, loga, ACT.Ln, bias=1.0).then_inc(gate_step, 1)
                elif j == 2:
                    for t in range(TT):
                        copied(kdec[:, t, :], full())
                    for t in range(TT):
                        copied(gv[:, t, 0:512], full())
                    copied(dec[:].rearrange("p h c -> p (h c)"), full()[:, 0:GH * 2 * TT], func=ACT.Exp, scale=1.0 / GTEMP)
                    for t in range(TT):
                        copied(loga[:, t, :], full(), func=ACT.Exp, scale=1.0 / GTEMP)
                elif j == 3:
                    for t in range(TT):
                        copied(gv[:, t, 512:1024], full())
                    for h in range(0, GH, 2):
                        copied(gqT[:, h:h + 2, :].rearrange("p h n -> p (h n)"), full(), scale=GDK ** -0.5)
                elif j == 4:
                    for half in range(2):
                        for t in range(TT):
                            copied(gr[:, t, half * 512:half * 512 + 512], full(), func=ACT.Silu)
                    act.wait_ge(o_full, TT * s + 1)
                    o_stats()
                elif j == 5:
                    copied(skT[:, :, CHUNK:], full().rearrange("p (f n) -> p f n", f=2))
                    copied(sv[:, 1:TT + 1, :], full().rearrange("p (t n) -> p t n", t=TT))
                    turn_o(0)
                    for f in range(0, 4, 2):
                        copied(sqT[:, f:f + 2, :].rearrange("p f n -> p (f n)"), full(), scale=HD ** -0.5)
                elif j == 6:
                    act.wait_ge(o_full, TT * s + 2)
                    o_stats()
                elif j == 7:
                    for f in range(4, 8, 2):
                        copied(sqT[:, f:f + 2, :].rearrange("p f n -> p (f n)"), full(), scale=HD ** -0.5)
                    turn_o(1)
                    after_vector(n)
                    sigmoids(0, 0)
                elif j == 8:
                    for q in range(2):
                        copied(ygl[:, q * 512:q * 512 + 512], full())
                    after_vector(n)
                    sigmoids(4, 4)
                    window_exps()
                elif j in (9, 10, 11):
                    after_vector(n)
                    if j == 9:
                        for q in range(2):
                            copied(ygl[:, q * 512:q * 512 + 512], full())
                    elif j == 10:
                        sigmoids(0, 8)
                    else:
                        sigmoids(4, 12)
                    window_out(j - 9)
                    window_exps()
                elif j == 12:
                    after_vector(n)
                    window_out(3)
                    for q in range(4):
                        copied(ysw[:, q * 512:q * 512 + 512], full())
                elif j == 13:
                    after_vector(n)
                    for q in range(2):
                        for t in range(TT):
                            copied(h2[:, t, q * 512:q * 512 + 512], full())
                elif j == 14:
                    after_vector(n)
                    root(stat_h[:, 1, :], stat_h[:, 0, :], D)
                else:
                    after_vector(n)
                    if j == 15:
                        for f in range(0, KT, 2):
                            copied(hT[:, f:f + 2, :].rearrange("p f n -> p (f n)"), full())
                    for q in [q for q in range(4) if SCORED[q] == j]:
                        b2 = q % 2
                        for f in range(0, 4, 2):
                            copied(pq[:, b2, f:f + 2, :].rearrange("p f n -> p (f n)"), full())
                        for t in range(TT):
                            copied(ysc[:, b2, t, :], full())

            def tail(n, i, j):
                after_vector(n)
                if j == 0:
                    act.wait_ge(x2_done, TT * (i + 1))
                    square_sums([(tX[:, t, :], stat_t[:, 0, t:t + 1]) for t in range(TT)])
                    root(stat_t[:, 1, 0:TT], stat_t[:, 0, 0:TT], D)
                elif j == 1:
                    for t in range(TT):
                        fn(ths[t], tX[:, t, :].rearrange("p (f n) -> p f n", n=P), ACT.Copy,
                           scale=stat_t[:, 2, t:t + 1]).then_inc(tail_scaled, 1)
                    for f in range(0, KT, 2):
                        b = full()
                        for g in range(2):
                            m = fn(thT[:, f + g, :], b[:, g * SEG:g * SEG + SEG], ACT.Copy, scale=g_ple[:, f + g:f + g + 1])
                        m.then_inc(emptied, 1)
                    for q in range(2):
                        for t in range(TT):
                            copied(tgate[:, t, q * 512:q * 512 + 512], full(), func=ACT.Sigmoid)
                    for q in range(2):
                        for t in range(TT):
                            copied(ths[t][:, 4 * q:4 * q + 4, :], full().rearrange("p (f n) -> p f n", n=P))
                else:
                    root(stat_t[:, 1, TT:2 * TT], stat_t[:, 0, TT:2 * TT], D)

            def peer_exp(m):
                act.wait_ge(topk_step, TK * m + 6)
                if m >= 2:
                    act.wait_ge(wts_step, 2 * (m - 1))
                fn(gexp[:, m % 2, :], tv[:], ACT.Exp, bias=negmax[:], accum_out=gsum[:, m % 2, :]).then_inc(topk_exp, 1)

            def peer_head(n):
                act.wait_ge(u_used, US + (n + 1) * TOPK)
                if n >= 2:
                    act.wait_ge(wts_step, 2 * (n - 1))
                fn(dots[:, n % 2, :], dots[:, n % 2, :], ACT.Gelu_apprx_tanh).then_inc(gelu_done, 1)
                act.wait_ge(wts_step, 2 * (n + 1))
                for kk in range(ODD):
                    m0 = n * ODD + kk
                    if m0 >= DS:
                        act.wait_ge(v_used_pe, VS // 2 + m0 - DS + 1)
                    fn(diag[:, m0 % DS, :], ident[:], ACT.Copy,
                       scale=dots[:, n % 2, 2 * kk + 1:2 * kk + 2]).then_inc(diag_done, 1)

            act.wait_ge(const_in, CONST_READY)
            act.wait_ge(setup, SETUP)
            for n in range(FIRST, LAST + 1):
                if 0 <= n + 1 < NHEAD:
                    peer_exp(n + 1)
                if 0 <= n < NHEAD:
                    peer_head(n)
                for kind, s, j in stages(n):
                    (front if kind == "front" else tail)(n, s, j)
                assert used.n == uses_through(n)

        @block.vector
        def _(dve):
            v = nc.vector
            steps = Count()
            roots = Count()

            def step(ins):
                steps.next()
                ins.then_inc(vec_step, 1)

            def settle():
                if steps.n:
                    dve.wait_ge(vec_step, steps.n)

            def inverse(dst, src):
                dve.wait_ge(root_done, roots.next())
                step(v.reciprocal(dst, src))

            def states(s, t):
                for half in range(2):
                    settle()
                    dve.wait_ge(u_full, 2 * TT * s + 2 * t + half + 1)
                    for h in range(GH):
                        step(v.scalar_tensor_tensor(
                            out=state[:, half, h, :], in0=state[:, 1 - half, h, :],
                            scalar=dec[:, h, 2 * t + half:2 * t + half + 1], in1=uw[half][:, h, :],
                            op0=ALU.mult, op1=ALU.add))

            def gated_o(t):
                inverse(gstat[:, 2, :], gstat[:, 1, :])
                settle()
                for h in range(GH):
                    step(v.scalar_tensor_tensor(
                        out=otok[:, h * GDV:h * GDV + GDV], in0=ow[:, h, :], scalar=gstat[:, 2, h:h + 1],
                        in1=gr[:, t, h * GDV:h * GDV + GDV], op0=ALU.mult, op1=ALU.mult))

            def biased(s, batch):
                dve.wait_ge(logit_full, 4 * s + batch + 1)
                first = s == 0 and batch < 2
                hd0 = (batch % 2) * 2 * GROUP
                for j in range(2 * GROUP):
                    slope = 2.0 ** (-8.0 * (hd0 + j + 1) / QH)
                    step(v.scalar_tensor_tensor(
                        out=sl[:, j, :], in0=dist[:, 0 if first else 1, :], scalar=-slope,
                        in1=wide[:, j // 2, (j % 2) * BAND:(j % 2) * BAND + BAND], op0=ALU.mult, op1=ALU.add))
                settle()
                step(v.tensor_reduce(sm[:, 0, :], sl, AX.X, ALU.max))
                settle()
                step(v.tensor_tensor(sm[:, 0, :], sm[:, 0, :], sinks[:, hd0:hd0 + 2 * GROUP], ALU.max))
                settle()
                step(v.tensor_tensor(sm[:, 2, :], sinks[:, hd0:hd0 + 2 * GROUP], sm[:, 0, :], ALU.subtract))
                step(v.tensor_scalar(sm[:, 1, :], sm[:, 0, :], -1.0, None, ALU.mult))

            def normed_probs(s, batch):
                dve.wait_ge(window_exp, WEXP * (4 * s + batch + 1))
                step(v.tensor_tensor(sm[:, 3, :], sm[:, 3, :], sm[:, 4, :], ALU.add))
                settle()
                step(v.reciprocal(sm[:, 4, :], sm[:, 3, :]))
                settle()
                step(v.tensor_tensor(probs[:, :, CHUNK:256], probs[:, :, CHUNK:256],
                                     sm[:, 4, :].unsqueeze(2).broadcast_to([P, 2 * GROUP, BAND]), ALU.mult))

            def largest(q):
                lists = []
                for t in range(TT):
                    for m in range(4):
                        h, half = 2 * q + m // 2, m % 2
                        lists.append((vals[:, t, h, half, :], lidx[:, t, h, half, :], ysc[:, q % 2, t, m * NK:m * NK + NK]))
                for c in (slice(0, 8), slice(8, 16)):
                    if c.start:
                        for val, _, row in lists:
                            step(v.match_replace(row, val[:, 0:8], row, LOW))
                        settle()
                    for val, _, row in lists:
                        step(v.max(val[:, c], row))
                    settle()
                    for val, at, row in lists:
                        step(v.max_index(at[:, c], val[:, c], row))
                    settle()

            def front(s, j):
                if j == 0:
                    inverse(stat_x[:, 2, :], stat_x[:, 1, :])
                elif j == 1:
                    dve.wait_ge(gate_step, 2 * (s + 1))
                    step(v.scalar_tensor_tensor(out=loga, in0=zs, scalar=0.0, in1=loga, op0=ALU.min, op1=ALU.subtract))
                elif j == 2:
                    step(v.tensor_tensor(kdec, kdec, loga, ALU.mult))
                elif j == 3:
                    states(s, 0)
                elif j == 4:
                    gated_o(0)
                elif j == 5:
                    states(s, 1)
                elif j == 6:
                    gated_o(1)
                elif j == 7:
                    biased(s, 0)
                elif j in (8, 9, 10):
                    normed_probs(s, j - 8)
                    biased(s, j - 7)
                    if j < 10:
                        q = j - 8
                        step(v.tensor_tensor(rD[:, q * 1024:q * 1024 + 1024], rE[:, q * 1024:q * 1024 + 1024], ygl, ALU.mult))
                elif j == 11:
                    normed_probs(s, 3)
                elif j == 12:
                    step(v.tensor_tensor(ysw, ysw, rE[:], ALU.mult))
                    if s + 1 < NSEG:
                        step(v.tensor_copy(skT[:, :, 0:CHUNK], skT[:, :, SEG:SEG + CHUNK]))
                        step(v.tensor_copy(sv[:, 0, :], sv[:, TT, :]))
                    settle()
                    step(v.tensor_tensor(rD[:], rD[:], ysw, ALU.add))
                elif j == 13:
                    dve.wait_ge(xres_in, 16 * (s + 1))
                    step(v.tensor_tensor(rX[:], rX[:], rC[:], ALU.add))
                    settle()
                    for t in range(TT):
                        step(v.scalar_tensor_tensor(out=h2[:, t, :], in0=xs[:, t, :], scalar=1.0, in1=xs[:, t, :],
                                                    op0=ALU.mult, op1=ALU.mult, accum_out=stat_h[:, 0, t:t + 1]))
                elif j == 14:
                    inverse(stat_h[:, 2, :], stat_h[:, 1, :])
                    settle()
                    for t in range(TT):
                        step(v.scalar_tensor_tensor(out=h2[:, t, :], in0=xs[:, t, :], scalar=stat_h[:, 2, t:t + 1],
                                                    in1=g_ffn[:], op0=ALU.mult, op1=ALU.mult))

                elif j >= 15:
                    for q in range(4):
                        if SCORED[q] == j:
                            largest(q)

            def tail(i, j):
                if j == 0:
                    inverse(stat_t[:, 2, 0:TT], stat_t[:, 1, 0:TT])
                elif j == 1:
                    xt = [tX[:, t, :].rearrange("p (f n) -> p f n", n=P) for t in range(TT)]
                    for t in range(TT):
                        step(v.tensor_tensor(ths[t], ths[t], tgate[:, t, :].rearrange("p (f n) -> p f n", n=P), ALU.mult))
                    settle()
                    for t in range(TT):
                        step(v.tensor_tensor(xt[t], xt[t], ths[t], ALU.add))
                    settle()
                    for t in range(TT):
                        step(v.scalar_tensor_tensor(out=ths[t], in0=xt[t], scalar=1.0, in1=xt[t], op0=ALU.mult,
                                                    op1=ALU.mult, accum_out=stat_t[:, 0, TT + t:TT + t + 1]))
                else:
                    inverse(stat_t[:, 2, TT:2 * TT], stat_t[:, 1, TT:2 * TT])
                    settle()
                    dve.wait_ge(gfin_in, 16 * (i + 1))
                    for t in range(TT):
                        step(v.scalar_tensor_tensor(out=tX[:, t, :], in0=tX[:, t, :], scalar=stat_t[:, 2, TT + t:TT + t + 1],
                                                    in1=g_fin, op0=ALU.mult, op1=ALU.mult))

            def stage_parts(n):
                dve.wait_ge(emptied, uses_through(n)) if uses_through(n) else None
                for kind, s, j in stages(n):
                    (front if kind == "front" else tail)(s, j)
                settle()
                dve.sem_inc(vec_done, 1)

            def topk(m, j):
                base = TK * m
                val = vals[:, m // NH % TT, m % NH]
                if base + j:
                    dve.wait_ge(topk_step, base + j)
                if j == 0:
                    ins = v.tensor_tensor(cand.rearrange("p (i j) -> p i j", i=TOPK),
                                          val[:, 0, :].unsqueeze(2).broadcast_to([P, TOPK, TOPK]),
                                          val[:, 1, :].unsqueeze(1).broadcast_to([P, TOPK, TOPK]), ALU.add)
                elif j == 1:
                    if m:
                        dve.wait_ge(topk_exp, m)
                    ins = v.max(tv[:, 0:8], cand)
                elif j == 2:
                    ins = v.max_index(pos[:, 0:8], tv[:, 0:8], cand)
                elif j == 3:
                    ins = v.match_replace(cand, tv[:, 0:8], cand, LOW)
                elif j == 4:
                    ins = v.max(tv[:, 8:16], cand)
                elif j == 5:
                    v.max_index(pos[:, 8:16], tv[:, 8:16], cand)
                    ins = v.tensor_scalar(negmax[:], tv[:, 0:1], -1.0, None, ALU.mult)
                elif j == 6:
                    v.tensor_scalar(posi[:, 0], pos[:], 4, None, ALU.logical_shift_right)
                    v.tensor_scalar(posi[:, 1], pos[:], 15, None, ALU.bitwise_and)
                    ins = v.tensor_copy(lidf[:], lidx[:, m // NH % TT, m % NH])
                elif j == 7:
                    ins = v.tensor_copy(posf[:], posi[:])
                elif j == 8:
                    ins = v.tensor_tensor(hot[:], iota16[:].unsqueeze(1).unsqueeze(1).broadcast_to([P, 2, TOPK, TOPK]),
                                          posf[:].unsqueeze(3).broadcast_to([P, 2, TOPK, TOPK]), ALU.is_equal)
                elif j == 9:
                    ins = v.tensor_tensor(hot[:], hot[:], lidf[:].unsqueeze(2).broadcast_to([P, 2, TOPK, TOPK]), ALU.mult)
                else:
                    ins = v.tensor_reduce(picked[:].rearrange("p q k -> p (q k)"),
                                          hot[:].rearrange("p q k i -> p (q k) i"), AX.X, ALU.add)
                ins.then_inc(topk_step, 1)

            def numbers(m):
                dve.wait_ge(topk_step, TK * (m + 1))
                if m >= 2:
                    dve.wait_ge(v_used_pe, VS // 2 + (m - 1) * ODD)
                    dve.wait_ge(v_used_dve, VS // 2 + (m - 1) * ODD)
                v.scalar_tensor_tensor(out=idx[:, m % 2, :], in0=picked[:, 0, :], scalar=float(NK),
                                       in1=picked[:, 1, :], op0=ALU.mult, op1=ALU.add).then_inc(idx_ready, 1)

            def norm_rows(i):
                dve.wait_ge(h_in, 16 * (i + 1))
                v.scalar_tensor_tensor(out=hbuf[:, i % 2, :], in0=hbuf[:, i % 2, :], scalar=stat_h[:, 2, i % TT:i % TT + 1],
                                       in1=g_ffn[:], op0=ALU.mult, op1=ALU.mult).then_inc(h_ready, 1)

            def dot(n, k):
                i = n // NH
                if n % NH == 0 and k == 0:
                    dve.wait_ge(h_ready, i + 1)
                if n >= 2 and k == 0:
                    dve.wait_ge(diag_done, (n - 1) * ODD)
                dve.wait_ge(u_in[k % US], (n * (TOPK // US) + k // US + 1) * 16)
                row = ubuf[:, k % US, :]
                v.scalar_tensor_tensor(out=row, in0=row, scalar=1.0, in1=hbuf[:, i % 2, :], op0=ALU.mult, op1=ALU.mult,
                                       accum_out=dots[:, n % 2, k:k + 1]).then_inc(u_used, 1)

            def weights(n):
                dve.wait_ge(topk_exp, n + 1)
                v.reciprocal(ginv[:, n % 2, :], gsum[:, n % 2, :]).then_inc(wts_step, 1)
                dve.wait_ge(gelu_done, n + 1)
                dve.wait_ge(wts_step, 2 * n + 1)
                v.scalar_tensor_tensor(out=dots[:, n % 2, :], in0=dots[:, n % 2, :], scalar=ginv[:, n % 2, :],
                                       in1=gexp[:, n % 2, :], op0=ALU.mult, op1=ALU.mult).then_inc(wts_step, 1)

            def add_row(n, kk):
                k = 2 * kk
                if n % NH == 0 and kk == 0:
                    dve.wait_ge(acc_in, 16 * (n // NH + 1))
                if kk == 0:
                    dve.wait_ge(wts_step, 2 * (n + 1))
                dve.wait_ge(v_used_dve, VS // 2 + n * ODD + kk)
                dve.wait_ge(v_in[k % VS], (n * (TOPK // VS) + k // VS + 1) * 16)
                v.scalar_tensor_tensor(out=acc[:], in0=vbuf[:, k % VS, :], scalar=dots[:, n % 2, k:k + 1], in1=acc[:],
                                       op0=ALU.mult, op1=ALU.add).then_inc(v_used_dve, 1)

            v.memset(eps[:], EPS).then_inc(setup, 1)
            v.memset(aT[:], 1.0).then_inc(setup, 1)
            v.memset(skT[:, :, 0:CHUNK], 0.0).then_inc(setup, 1)
            v.memset(sv[:, 0, :], 0.0).then_inc(setup, 1)
            v.memset(probs[:], 0.0).then_inc(setup, 1)
            v.memset(state[:, 1], 0.0).then_inc(setup, 1)
            dve.sem_inc(u_used, US)
            dve.sem_inc(v_used_dve, VS // 2)
            dve.sem_inc(v_used_pe, VS // 2)
            dve.wait_ge(setup, SETUP)
            dve.wait_ge(const_in, CONST_READY)
            for n in range(FIRST, LAST + 1):
                peer = 0 <= n < NHEAD
                find = 0 <= n + 1 < NHEAD
                for k in range(TOPK):
                    if peer:
                        dot(n, k)
                    if find and k < TK:
                        topk(n + 1, k)
                if find:
                    numbers(n + 1)
                if peer:
                    weights(n)
                    for kk in range(ODD // 2):
                        add_row(n, kk)
                if n > FIRST:
                    stage_parts(n - 1)
                if find and (n + 1) % NH == 0:
                    norm_rows((n + 1) // NH)
                if peer:
                    for kk in range(ODD // 2, ODD):
                        add_row(n, kk)
                    if n % NH == NH - 1:
                        dve.wait_ge(v_used_dve, VS // 2 + (n + 1) * ODD)
                        dve.wait_ge(v_used_pe, VS // 2 + (n + 1) * ODD)
                        i = n // NH
                        if i >= TT:
                            dve.wait_ge(tail_out, 16 * (i // TT))
                        v.tensor_tensor(tX[:, i % TT, :].rearrange("p (c n) -> p c n", c=2), acc[:].rearrange("p (c n) -> p c n", c=2),
                                        ysum[:], ALU.add).then_inc(x2_done, 1)


WEXP = 2 * GROUP + 1


def shape_tables():
    q = np.arange(P)[:, None]
    k = np.arange(P)[None, :]
    tri = ((q // CHUNK == k // CHUNK) & (q > k)).astype(np.float32)
    chunk_of = (q // CHUNK == np.arange(2)[None, :]).astype(np.float32)
    col = np.arange(BAND)[None, :]
    near = (col // CHUNK == q // CHUNK) | (col // CHUNK == q // CHUNK + 1)
    far = np.abs(q - (col - CHUNK)).astype(np.float32)
    later = np.where(near, far, FAR).astype(np.float32)
    first = np.where(near & (col >= CHUNK), far, FAR).astype(np.float32)
    return {"ident": np.eye(P, dtype=np.float32), "tri": tri, "chunk_of": chunk_of,
            "dist": np.stack([first, later], 1), "iota16": np.arange(TOPK, dtype=np.float32)}


def kernel(**inputs):
    import concourse.bacc as bacc
    from concourse.bass_utils import run_bass_kernel_spmd

    a = {k: np.asarray(v) for k, v in inputs.items()}

    def feature_major(g, n):
        return np.ascontiguousarray(g.reshape(n, P).T)

    def by_rows(w):
        return w.reshape(-1, P, w.shape[1]).transpose(1, 0, 2).reshape(P, -1)

    w = a["w_in"][0]
    at = np.cumsum([0, 512, 512, 1024, 1024, GRANK, 1024, 256, 256])
    gq, gk, gvw, grw, ga, sq, sk, svw = (w[:, at[i]:at[i + 1]] for i in range(8))
    order = [4 * (2 * (f // GROUP) + half) + f % GROUP for f in range(8) for half in range(2)]
    sq = sq.reshape(D, QH, HD)[:, order].reshape(D, D)
    swo = a["w_swa_out"][0].reshape(QH, HD, D)[order].reshape(D, D)
    bg, glo, wo, wq, pg = a["w_branch_gate"][0], a["w_gla_out"][0], a["w_out"][0], a["peer_wq"][0], a["w_ple_gate"][0]
    H = 512
    parts = {"gk": gk, "gv0": gvw[:, :H], "gv1": gvw[:, H:], "gq": gq, "gr0": grw[:, :H], "gr1": grw[:, H:],
             "kv": np.concatenate([sk, svw], 1), "sq0": sq[:, :H], "sq1": sq[:, H:]}
    for q in range(2):
        c = slice(q * H, q * H + H)
        parts.update({f"bgg{q}": bg[:, c], f"bgs{q}": bg[:, D + q * H:D + q * H + H], f"glo{q}": glo[:, c],
                      f"swo{q}": swo[:, c], f"wo{q}": wo[:, c], f"pg{q}": pg[:, c]})
    for q in range(4):
        parts[f"wq{q}"] = wq[:, q * H:q * H + H]
    slabs = np.zeros((len(SLABS), P, KT * SW), np.float32)
    for n, name in enumerate(SLABS):
        if name == "pp":
            slabs[n, :, :2048] = by_rows(a["w_ple_proj"][0])
        else:
            slabs[n] = by_rows(parts[name])

    arrays = {
        "x": a["x"].reshape(SEQ, D), "slabs": slabs,
        "pT": a["p"].reshape(SEQ, 2, P).transpose(2, 1, 0),
        "g_mix": feature_major(a["norm_mix"][0], KT), "g_ple": feature_major(a["norm_ple"][0], KT),
        "g_on": feature_major(a["gla_onorm"][0], 2), "b_bg": feature_major(a["b_branch_gate"][0], 2 * KT),
        "sinks": a["swa_sinks"][0], "g_ffn": a["norm_ffn"][0], "g_fin": a["norm_final"],
        "wga": by_rows(ga).reshape(P, KT, GRANK),
        "wa2": np.concatenate([a["w_gla_a2"][0], a["b_gla_a"]], 0),
        "subk": a["peer_subkeys"][0].transpose(2, 0, 1),
        "u": a["peer_u"][0], "v": a["peer_v"][0], **shape_tables(),
    }
    arrays = {k: np.ascontiguousarray(v) for k, v in arrays.items()}
    nc = bacc.Bacc("TRN2", target_bir_lowering=False, num_devices=1)
    aps = {k: nc.dram_tensor(f"in_{k}", v.shape, F32, kind="ExternalInput").ap() for k, v in arrays.items()}
    out = nc.dram_tensor("out_0", (SEQ, D), F32, kind="ExternalOutput").ap()
    build(nc, aps, out)
    r = run_bass_kernel_spmd(nc, [{f"in_{k}": v for k, v in arrays.items()}], core_ids=[0])
    return r.results[0]["out_0"].reshape(1, SEQ, D)
```
